# Optimizing a Trainium2 kernel written in Bass

```python
import math
import jax, jax.numpy as jnp
from jax import lax
import numpy as np

D_MODEL = 1024
BATCH = 1
SEQ = 256
DEPTH = 2
DEC_BATCH = 8
DEC_SEQ = 8
PAST_LEN = 2048
PAGE_SIZE = 128

MIX_W = D_MODEL
GROUP_W = MIX_W // 4
HEAD_DIM = 64
N_HEADS = GROUP_W // HEAD_DIM
RWKV_DECAY_RANK = 32
RWKV_ICL_RANK = 32
RWKV_GATE_RANK = 64
RWKV_GN_EPS = 64e-5
RWKV_COLS = 3 * GROUP_W + RWKV_DECAY_RANK + RWKV_ICL_RANK + RWKV_GATE_RANK
CONV_K = 4
RG_BLOCKS = N_HEADS
RG_BLOCK_W = GROUP_W // RG_BLOCKS
RG_C = 8.0
RG_COLS = 2 * GROUP_W
GDN_COLS = 4 * GROUP_W + 2 * N_HEADS
GLA_DK = HEAD_DIM // 2
GLA_GATE_RANK = 16
GLA_TAU = 16.0
GLA_COLS = 2 * N_HEADS * GLA_DK + 2 * GROUP_W + GLA_GATE_RANK
IN_COLS = RWKV_COLS + RG_COLS + GDN_COLS + GLA_COLS
D_FF = ((8 * D_MODEL // 3 + 127) // 128) * 128
CHUNK = 64
NORM_EPS = 1e-6

IN_SPLITS = [RWKV_COLS, RWKV_COLS + RG_COLS, RWKV_COLS + RG_COLS + GDN_COLS]
RWKV_SPLITS = [GROUP_W, 2 * GROUP_W, 3 * GROUP_W, 3 * GROUP_W + RWKV_DECAY_RANK,
               3 * GROUP_W + RWKV_DECAY_RANK + RWKV_ICL_RANK]
GDN_SPLITS = [3 * GROUP_W, 4 * GROUP_W, 4 * GROUP_W + N_HEADS]
GLA_SPLITS = [N_HEADS * GLA_DK, 2 * N_HEADS * GLA_DK, 2 * N_HEADS * GLA_DK + GROUP_W,
              2 * N_HEADS * GLA_DK + 2 * GROUP_W]

kernel_name = 'hybrid_rwkv7_rglru_gdn_gla_macaron_step'

F32 = jnp.float32

def _rmsnorm(x, w):
    xf = x.astype(F32)
    y = xf * lax.rsqrt(jnp.mean(xf * xf, axis=-1, keepdims=True) + NORM_EPS)
    return (y * w.astype(F32)).astype(x.dtype)

def _head_rmsnorm(x, w):
    return x * lax.rsqrt(jnp.mean(x * x, axis=-1, keepdims=True) + NORM_EPS) * w

def _l2norm(x):
    return x * lax.rsqrt(jnp.sum(x * x, axis=-1, keepdims=True) + 1e-12)

def _heads(t, d):
    return t.reshape(t.shape[0], t.shape[1], -1, d)

def _swiglu(x, w_gate, w_up, w_down):
    return (jax.nn.silu(x @ w_gate) * (x @ w_up)) @ w_down

def _causal_conv(x, buf, w):
    xp = jnp.concatenate([buf.astype(x.dtype), x], axis=1)
    y = lax.conv_general_dilated(xp, w.astype(x.dtype)[:, None, :], window_strides=(1,), padding='VALID',
                                 dimension_numbers=('NWC', 'WIO', 'NWC'), feature_group_count=x.shape[-1])
    return y, xp[:, -(CONV_K - 1):]

def _linear_scan(a, b, h0):
    b = b.at[:, 0].add(a[:, 0] * h0)
    def comb(l, r):
        return (l[0] * r[0], r[0] * l[1] + r[1])
    _, h = lax.associative_scan(comb, (a, b), axis=1)
    return h

def _chunk_len(T):
    return CHUNK if T % CHUNK == 0 else T

def _to_chunks(x, L):
    B, T, H, d = x.shape
    return x.reshape(B, T // L, L, H, d).transpose(1, 0, 3, 2, 4)

def _from_chunks(y):
    n, B, H, L, d = y.shape
    return y.transpose(1, 0, 3, 2, 4).reshape(B, n * L, H, d)

def _rwkv7_scan(r, w, k, v, kk, a, S0):
    def step(S, inp):
        r_t, w_t, k_t, v_t, kk_t, a_t = inp
        sa = jnp.einsum('bhij,bhj->bhi', S, -kk_t)
        S = (S * w_t[:, :, None, :] + sa[..., None] * (kk_t * a_t)[:, :, None, :]
             + v_t[..., None] * k_t[:, :, None, :])
        return S, jnp.einsum('bhij,bhj->bhi', S, r_t)
    xs = tuple(t.transpose(1, 0, 2, 3) for t in (r, w, k, v, kk, a))
    S, ys = lax.scan(step, S0, xs)
    return ys.transpose(1, 0, 2, 3), S

def _gated_delta_chunked(q, k, v, beta, g, S0):
    L = _chunk_len(q.shape[1])
    dk = q.shape[-1]
    qc, kc, vc = (_to_chunks(t, L) for t in (q, k, v))
    bc = _to_chunks(beta[..., None], L)[..., 0]
    gc = _to_chunks(g[..., None], L)[..., 0]
    strict = jnp.tril(jnp.ones((L, L), bool), -1)
    incl = jnp.tril(jnp.ones((L, L), bool))
    eye = jnp.eye(L, dtype=F32)

    def step(S, inp):
        qi, ki, vi, bi, gi = inp
        G = jnp.cumsum(gi, axis=-1)
        diff = G[..., :, None] - G[..., None, :]
        eG = jnp.exp(G)
        kk = jnp.einsum('bhid,bhjd->bhij', ki, ki)
        A = bi[..., :, None] * kk * jnp.exp(jnp.where(strict, diff, -jnp.inf))
        rhs = jnp.concatenate([(bi * eG)[..., None] * ki, bi[..., None] * vi], axis=-1)
        sol = lax.linalg.triangular_solve(eye + A, rhs, left_side=True, lower=True, unit_diagonal=True)
        W, U = sol[..., :dk], sol[..., dk:]
        v_new = U - jnp.einsum('bhld,bhde->bhle', W, S)
        attn = jnp.einsum('bhid,bhjd->bhij', qi, ki) * jnp.exp(jnp.where(incl, diff, -jnp.inf))
        o = jnp.einsum('bhld,bhde->bhle', qi * eG[..., None], S) + jnp.einsum('bhij,bhje->bhie', attn, v_new)
        G_last = G[..., -1:]
        S_new = (jnp.exp(G_last)[..., None] * S
                 + jnp.einsum('bhld,bhle->bhde', ki * jnp.exp(G_last - G)[..., None], v_new))
        return S_new, o

    S, oc = lax.scan(step, S0, (qc, kc, vc, bc, gc))
    return _from_chunks(oc), S

def _gla_chunked(q, k, v, gk, S0):
    L = _chunk_len(q.shape[1])
    qc, kc, vc, gc = (_to_chunks(t, L) for t in (q, k, v, gk))
    incl = jnp.tril(jnp.ones((L, L), bool))[:, :, None]

    def step(S, inp):
        qi, ki, vi, gi = inp
        Bc = jnp.cumsum(gi, axis=2)
        diff = Bc[:, :, :, None, :] - Bc[:, :, None, :, :]
        decay = jnp.exp(jnp.where(incl, diff, -jnp.inf))
        attn = jnp.einsum('bhid,bhjd,bhijd->bhij', qi, ki, decay)
        o = jnp.einsum('bhid,bhde->bhie', qi * jnp.exp(Bc), S) + jnp.einsum('bhij,bhje->bhie', attn, vi)
        B_last = Bc[:, :, -1:, :]
        S_new = (jnp.exp(B_last[:, :, 0, :])[..., None] * S
                 + jnp.einsum('bhld,bhle->bhde', ki * jnp.exp(B_last - Bc), vi))
        return S_new, o

    S, oc = lax.scan(step, S0, (qc, kc, vc, gc))
    return _from_chunks(oc), S

def _rwkv7_group(p, shift0, S0, lp):
    B, T, _ = p.shape
    prev = jnp.concatenate([shift0.astype(F32)[:, None], p[:, :-1]], axis=1)
    xm = p + (prev - p) * lp['rwkv_mu']
    r, k, v, xw, xa, xg = jnp.split(xm, RWKV_SPLITS, axis=-1)
    w = -jax.nn.softplus(-(lp['rwkv_w0'] + jnp.tanh(xw) @ lp['rwkv_w2'])) - 0.5
    decay = jnp.exp(-jnp.exp(w))
    a = jax.nn.sigmoid(lp['rwkv_a0'] + xa @ lp['rwkv_a2'])
    g = jax.nn.sigmoid(xg) @ lp['rwkv_g2']
    kk = _l2norm(_heads(k * lp['rwkv_k_k'], HEAD_DIM))
    k = k * (1.0 + (a - 1.0) * lp['rwkv_k_a'])
    rh, kh, vh, ah, wh = (_heads(t, HEAD_DIM) for t in (r, k, v, a, decay))
    y, S = _rwkv7_scan(rh, wh, kh, vh, kk, ah, S0.astype(F32))
    mu = jnp.mean(y, axis=-1, keepdims=True)
    var = jnp.mean(jnp.square(y - mu), axis=-1, keepdims=True)
    y = ((y - mu) * lax.rsqrt(var + RWKV_GN_EPS)).reshape(B, T, GROUP_W) * lp['rwkv_ln_w'] + lp['rwkv_ln_b']
    bonus = jnp.sum(rh * kh * lp['rwkv_r_k'], axis=-1, keepdims=True) * vh
    out = (y + bonus.reshape(B, T, GROUP_W)) * g
    return out, p[:, -1], S

def _rglru_group(p, conv0, h0, lp):
    B, T, _ = p.shape
    xb, gate = jnp.split(p, [GROUP_W], axis=-1)
    xc, conv_new = _causal_conv(xb, conv0, lp['rg_conv_w'])
    xc = xc + lp['rg_conv_b']
    xh = xc.reshape(B, T, RG_BLOCKS, RG_BLOCK_W)
    r = jax.nn.sigmoid(jnp.einsum('btni,nij->btnj', xh, lp['rg_wa']).reshape(B, T, GROUP_W) + lp['rg_ba'])
    i = jax.nn.sigmoid(jnp.einsum('btni,nij->btnj', xh, lp['rg_wx']).reshape(B, T, GROUP_W) + lp['rg_bx'])
    log_a = -RG_C * r * jax.nn.softplus(-lp['rg_lambda'].astype(F32))
    a = jnp.exp(log_a)
    b = jnp.sqrt(-jnp.expm1(2.0 * log_a)) * (i * xc)
    h = _linear_scan(a, b, h0.astype(F32))
    return h * jax.nn.gelu(gate), conv_new, h[:, -1]

def _gdn_group(p, conv0, S0, lp):
    B, T, _ = p.shape
    qkv, z, b, a = jnp.split(p, GDN_SPLITS, axis=-1)
    qkv, conv_new = _causal_conv(qkv, conv0, lp['gdn_conv_w'])
    q, k, v = jnp.split(jax.nn.silu(qkv), [GROUP_W, 2 * GROUP_W], axis=-1)
    q = _l2norm(_heads(q, HEAD_DIM)) * (HEAD_DIM ** -0.5)
    k = _l2norm(_heads(k, HEAD_DIM))
    v = _heads(v, HEAD_DIM)
    beta = jax.nn.sigmoid(b)
    g = -jnp.exp(lp['gdn_A_log'].astype(F32)) * jax.nn.softplus(a + lp['gdn_dt_bias'])
    o, S = _gated_delta_chunked(q, k, v, beta, g, S0.astype(F32))
    o = _head_rmsnorm(o, lp['gdn_norm_w']) * jax.nn.silu(_heads(z, HEAD_DIM))
    return o.reshape(B, T, GROUP_W), conv_new, S

def _gla_group(p, S0, lp):
    B, T, _ = p.shape
    q, k, v, gt, gd = jnp.split(p, GLA_SPLITS, axis=-1)
    gk = jax.nn.log_sigmoid(gd @ lp['gla_g2'] + lp['gla_gb']) / GLA_TAU
    q = _heads(q, GLA_DK) * (GLA_DK ** -0.5)
    o, S = _gla_chunked(q, _heads(k, GLA_DK), _heads(v, HEAD_DIM), _heads(gk, GLA_DK), S0.astype(F32))
    o = _head_rmsnorm(o, lp['gla_norm_w']) * jax.nn.silu(_heads(gt, HEAD_DIM))
    return o.reshape(B, T, GROUP_W), S

def _trunk_layer(x, lp, st):
    rw_shift, rw_S, rg_conv, rg_h, gdn_conv, gdn_S, gla_S = st
    x = x + 0.5 * _swiglu(_rmsnorm(x, lp['norm_ffn1']), lp['ffn1_gate'], lp['ffn1_up'], lp['ffn1_down'])
    h = _rmsnorm(x, lp['norm_mix'])
    proj = (h @ lp['w_in']).astype(F32)
    p_rw, p_rg, p_gdn, p_gla = jnp.split(proj, IN_SPLITS, axis=-1)
    o_rw, rw_shift, rw_S = _rwkv7_group(p_rw, rw_shift, rw_S, lp)
    o_rg, rg_conv, rg_h = _rglru_group(p_rg, rg_conv, rg_h, lp)
    o_gdn, gdn_conv, gdn_S = _gdn_group(p_gdn, gdn_conv, gdn_S, lp)
    o_gla, gla_S = _gla_group(p_gla, gla_S, lp)
    mixed = jnp.concatenate([o_rw, o_rg, o_gdn, o_gla], axis=-1).astype(x.dtype)
    x = x + mixed @ lp['w_out']
    x = x + 0.5 * _swiglu(_rmsnorm(x, lp['norm_ffn2']), lp['ffn2_gate'], lp['ffn2_up'], lp['ffn2_down'])
    return x, (rw_shift, rw_S, rg_conv, rg_h, gdn_conv, gdn_S, gla_S)

def _zero_state(batch, dtype):
    return (jnp.zeros((batch, RWKV_COLS), dtype),
            jnp.zeros((batch, N_HEADS, HEAD_DIM, HEAD_DIM), dtype),
            jnp.zeros((batch, CONV_K - 1, GROUP_W), dtype),
            jnp.zeros((batch, GROUP_W), dtype),
            jnp.zeros((batch, CONV_K - 1, 3 * GROUP_W), dtype),
            jnp.zeros((batch, N_HEADS, HEAD_DIM, HEAD_DIM), dtype),
            jnp.zeros((batch, N_HEADS, GLA_DK, HEAD_DIM), dtype))

def _run_trunk(x, layer_states, lps, norm_final):
    new = []
    for i in range(DEPTH):
        x, st = _trunk_layer(x, lps[i], layer_states[i])
        new.append(st)
    stacked = tuple(jnp.stack([new[i][j] for i in range(DEPTH)]).astype(x.dtype) for j in range(len(new[0])))
    return _rmsnorm(x, norm_final), stacked

def setup_inputs(seed: int = 0) -> dict:
    key = jax.random.key(seed)
    ks = iter(jax.random.split(key, 96))
    def nrm(shape, scale):
        return jax.random.normal(next(ks), shape, F32) * scale
    def uni(shape, lo, hi):
        return jax.random.uniform(next(ks), shape, F32, lo, hi)
    def gains(shape):
        return 1.0 + nrm(shape, 0.02)
    L, G, H, N = DEPTH, GROUP_W, N_HEADS, HEAD_DIM
    lam_a = uni((L, G), 0.9, 0.999)
    dt = jnp.exp(uni((L, H), math.log(1e-3), math.log(1e-1)))
    return {
        'x_prompt': nrm((BATCH, SEQ, D_MODEL), 1.0),
        'x_sample': nrm((DEC_BATCH, DEC_SEQ, D_MODEL), 1.0),
        'state_rwkv_shift': nrm((L, DEC_BATCH, RWKV_COLS), 1.0),
        'state_rwkv_wkv': nrm((L, DEC_BATCH, H, N, N), 0.3),
        'state_rglru_conv': nrm((L, DEC_BATCH, CONV_K - 1, G), 1.0),
        'state_rglru_h': nrm((L, DEC_BATCH, G), 0.5),
        'state_gdn_conv': nrm((L, DEC_BATCH, CONV_K - 1, 3 * G), 1.0),
        'state_gdn_S': nrm((L, DEC_BATCH, H, N, N), 0.3),
        'state_gla_S': nrm((L, DEC_BATCH, H, GLA_DK, N), 0.3),
        'norm_ffn1': gains((L, D_MODEL)),
        'ffn1_gate': nrm((L, D_MODEL, D_FF), D_MODEL ** -0.5),
        'ffn1_up': nrm((L, D_MODEL, D_FF), D_MODEL ** -0.5),
        'ffn1_down': nrm((L, D_FF, D_MODEL), D_FF ** -0.5),
        'norm_mix': gains((L, D_MODEL)),
        'w_in': nrm((L, D_MODEL, IN_COLS), D_MODEL ** -0.5),
        'w_out': nrm((L, MIX_W, D_MODEL), MIX_W ** -0.5),
        'rwkv_mu': uni((L, RWKV_COLS), 0.0, 1.0),
        'rwkv_w0': uni((L, G), -6.0, 1.0),
        'rwkv_w2': nrm((L, RWKV_DECAY_RANK, G), 0.1 * RWKV_DECAY_RANK ** -0.5),
        'rwkv_a0': nrm((L, G), 0.1),
        'rwkv_a2': nrm((L, RWKV_ICL_RANK, G), 0.1 * RWKV_ICL_RANK ** -0.5),
        'rwkv_g2': nrm((L, RWKV_GATE_RANK, G), RWKV_GATE_RANK ** -0.5),
        'rwkv_k_k': 0.85 + nrm((L, G), 0.02),
        'rwkv_k_a': gains((L, G)),
        'rwkv_r_k': nrm((L, H, N), 0.1),
        'rwkv_ln_w': gains((L, G)),
        'rwkv_ln_b': nrm((L, G), 0.02),
        'rg_conv_w': nrm((L, CONV_K, G), CONV_K ** -0.5),
        'rg_conv_b': nrm((L, G), 0.02),
        'rg_wa': nrm((L, RG_BLOCKS, RG_BLOCK_W, RG_BLOCK_W), RG_BLOCK_W ** -0.5),
        'rg_ba': nrm((L, G), 0.02),
        'rg_wx': nrm((L, RG_BLOCKS, RG_BLOCK_W, RG_BLOCK_W), RG_BLOCK_W ** -0.5),
        'rg_bx': nrm((L, G), 0.02),
        'rg_lambda': jnp.log(lam_a) - jnp.log1p(-lam_a),
        'gdn_conv_w': nrm((L, CONV_K, 3 * G), CONV_K ** -0.5),
        'gdn_A_log': jnp.log(uni((L, H), 1.0, 16.0)),
        'gdn_dt_bias': dt + jnp.log(-jnp.expm1(-dt)),
        'gdn_norm_w': gains((L, N)),
        'gla_g2': nrm((L, GLA_GATE_RANK, H * GLA_DK), GLA_GATE_RANK ** -0.5),
        'gla_gb': nrm((L, H * GLA_DK), 0.1),
        'gla_norm_w': gains((L, N)),
        'norm_ffn2': gains((L, D_MODEL)),
        'ffn2_gate': nrm((L, D_MODEL, D_FF), D_MODEL ** -0.5),
        'ffn2_up': nrm((L, D_MODEL, D_FF), D_MODEL ** -0.5),
        'ffn2_down': nrm((L, D_FF, D_MODEL), D_FF ** -0.5),
        'norm_final': gains((D_MODEL,)),
    }

def reference(x_prompt, x_sample, state_rwkv_shift, state_rwkv_wkv, state_rglru_conv, state_rglru_h,
              state_gdn_conv, state_gdn_S, state_gla_S, norm_ffn1, ffn1_gate, ffn1_up, ffn1_down,
              norm_mix, w_in, w_out, rwkv_mu, rwkv_w0, rwkv_w2, rwkv_a0, rwkv_a2, rwkv_g2, rwkv_k_k,
              rwkv_k_a, rwkv_r_k, rwkv_ln_w, rwkv_ln_b, rg_conv_w, rg_conv_b, rg_wa, rg_ba, rg_wx, rg_bx,
              rg_lambda, gdn_conv_w, gdn_A_log, gdn_dt_bias, gdn_norm_w, gla_g2, gla_gb, gla_norm_w,
              norm_ffn2, ffn2_gate, ffn2_up, ffn2_down, norm_final):
    stacked = dict(norm_ffn1=norm_ffn1, ffn1_gate=ffn1_gate, ffn1_up=ffn1_up, ffn1_down=ffn1_down,
                   norm_mix=norm_mix, w_in=w_in, w_out=w_out, rwkv_mu=rwkv_mu, rwkv_w0=rwkv_w0,
                   rwkv_w2=rwkv_w2, rwkv_a0=rwkv_a0, rwkv_a2=rwkv_a2, rwkv_g2=rwkv_g2, rwkv_k_k=rwkv_k_k,
                   rwkv_k_a=rwkv_k_a, rwkv_r_k=rwkv_r_k, rwkv_ln_w=rwkv_ln_w, rwkv_ln_b=rwkv_ln_b,
                   rg_conv_w=rg_conv_w, rg_conv_b=rg_conv_b, rg_wa=rg_wa, rg_ba=rg_ba, rg_wx=rg_wx,
                   rg_bx=rg_bx, rg_lambda=rg_lambda, gdn_conv_w=gdn_conv_w, gdn_A_log=gdn_A_log,
                   gdn_dt_bias=gdn_dt_bias, gdn_norm_w=gdn_norm_w, gla_g2=gla_g2, gla_gb=gla_gb,
                   gla_norm_w=gla_norm_w, norm_ffn2=norm_ffn2, ffn2_gate=ffn2_gate, ffn2_up=ffn2_up,
                   ffn2_down=ffn2_down)
    lps = [{name: arr[i] for name, arr in stacked.items()} for i in range(DEPTH)]

    prompt_states = [_zero_state(x_prompt.shape[0], x_prompt.dtype) for _ in range(DEPTH)]
    y_prompt, new_p = _run_trunk(x_prompt, prompt_states, lps, norm_final)
    p_rwkv_shift, p_rwkv_wkv, p_rglru_conv, p_rglru_h, p_gdn_conv, p_gdn_S, p_gla_S = new_p

    sample_in = (state_rwkv_shift, state_rwkv_wkv, state_rglru_conv, state_rglru_h,
                 state_gdn_conv, state_gdn_S, state_gla_S)
    sample_states = [tuple(s[i] for s in sample_in) for i in range(DEPTH)]
    y_sample, new_s = _run_trunk(x_sample, sample_states, lps, norm_final)
    s_rwkv_shift, s_rwkv_wkv, s_rglru_conv, s_rglru_h, s_gdn_conv, s_gdn_S, s_gla_S = new_s

    return (y_prompt, y_sample,
            p_rwkv_shift, p_rwkv_wkv, p_rglru_conv, p_rglru_h, p_gdn_conv, p_gdn_S, p_gla_S,
            s_rwkv_shift, s_rwkv_wkv, s_rglru_conv, s_rglru_h, s_gdn_conv, s_gdn_S, s_gla_S)


_drawn_inputs = setup_inputs


def setup_inputs(seed=0):
    import zlib

    import numpy as np

    out = dict(_drawn_inputs(seed))
    spreads = {}
    factors = {'norm_ffn1': 3.399,
     'rwkv_w2': 8.0,
     'rwkv_k_k': 7.679,
     'rwkv_ln_w': 29.634,
     'rwkv_ln_b': 28.108,
     'rg_ba': 8.0,
     'rg_bx': 6.059,
     'gdn_norm_w': 27.699,
     'gla_norm_w': 21.773,
     'norm_ffn2': 5.051,
     'norm_final': 8.088,
     'rwkv_r_k': 2.703}
    for name, (base, spread) in spreads.items():
        noise = np.random.default_rng([zlib.crc32(name.encode()), seed]).standard_normal(out[name].shape)
        drawn = base * np.exp(spread * noise) if base else spread * noise
        out[name] = __import__('jax').numpy.asarray(drawn.astype(out[name].dtype))
    for name, factor in factors.items():
        out[name] = (out[name] * factor).astype(out[name].dtype)
    return out
```

```python
from contextlib import ExitStack

import numpy as np

import concourse.bass as bass
from concourse import mybir

F32, F32R, U32 = mybir.dt.float32, mybir.dt.float32r, mybir.dt.uint32
ACT = mybir.ActivationFunctionType
ALU = mybir.AluOpType

D, DEPTH, SEQ, DECB, DECT = 1024, 2, 256, 8, 8
TOK = SEQ + DECB * DECT
GW, HD, NH, DK = 256, 64, 4, 32
CH = 64
NC = TOK // CH
DEC = NC - 1
FF = 2816
KT, FT = D // 128, FF // 128
NSEQ = 1 + DECB
CONV = 4
GNE = 64e-5
WDEC = float(np.exp(-0.5))
GLA_TAU = 16.0

RING = 4
FFN_UNITS = 3 * FT
IN_TILES = 26
IN0 = FFN_UNITS
OUT0 = IN0 + IN_TILES
FFN2 = OUT0 + KT
UNITS = FFN2 + FFN_UNITS
assert FFN2 % RING == 0 and (2 * FT) % RING == 0

RW_COLS, RG_COLS, GDN_COLS = 3 * GW + 128, 2 * GW, 4 * GW + 2 * NH
RG0, GDN0, GLA0 = RW_COLS, RW_COLS + RG_COLS, RW_COLS + RG_COLS + GDN_COLS
GLA_GD = GLA0 + 2 * NH * DK + 2 * GW
T_RW, T_GDN, T_SMALL, T_Z, T_GLA, T_GT, T_RG, T_RGG = 0, 7, 13, 14, 16, 20, 22, 24
TILE_COL = ([128 * i for i in range(7)] + [GDN0 + 128 * i for i in range(6)] + [None]
            + [GDN0 + 3 * GW + 128 * i for i in range(2)] + [GLA0 + 128 * i for i in range(6)]
            + [RG0 + 128 * i for i in range(4)])


def columns(spec):
    at, out = 0, {}
    for name, n in spec:
        out[name] = (at, n)
        at += n
    return out, at


PAR, PARN = columns([
    ("n1", 8), ("nm", 8), ("n2", 8), ("mu", 7), ("w0", 2), ("a0", 2), ("kk", 2), ("ka", 2), ("rk", 2),
    ("lnw", 2), ("lnb", 2), ("rgcw", 8), ("rgcb", 2), ("ba", 2), ("bx", 2), ("lam", 2), ("gcw", 24),
    ("gnw", 1), ("glw", 1), ("alog", 1), ("dtb", 1), ("gb", 1), ("lora", 256), ("glag", 256),
    ("wa", 128), ("wx", 128)])
CST, CSTN = columns([
    ("hones", 128), ("ones", 128), ("tri", 256),
    ("lev", 7 * 64), ("cmask", TOK), ("seqm", 8), ("e6", 1), ("e12", 1), ("gne", 1),
    ("one", 1), ("nf", 8)])
SIN, SINN = columns([("shift", 7 * 8), ("rgc", 2 * 8 * 3), ("h", 2 * 8), ("gc", 6 * 8 * 3)])
SOUT, SOUTN = columns([("shift", 7 * 9), ("rgc", 2 * 9 * 3), ("h", 2 * 9), ("gc", 6 * 9 * 3)])
MST, MSTN = columns([("rw", 2 * NSEQ * 64), ("gdn", 2 * NSEQ * 64), ("gla", NSEQ * 64)])

RWP = 1 + SEQ + DECB * (1 + DECT)
CVP = 3 + SEQ + DECB * (3 + DECT)


MIX_SIGNALS = {
    "pads": 1, "chain_zero": 1, "xm": 7, "lora_in": 1, "lora_mm": 3, "sg": 2, "ra": 2,
    "rw_gc": 2, "shift_kept": 1, "kkraw": 2, "kk_sq": 1, "rkr": 2, "kk_sum": 1, "rk_sum": 1, "cum": 2, "prev": 1,
    "rw_P": 1, "kk_rn": 1, "rb": 1, "rw_ops": 1, "kPi": 1, "bPi": 1, "bonus": 1, "kbL": 4,
    "rw_pairs": 2, "rw_pairs_read": 6,
    "rw_rows_mm": 3, "rw_rows": 1, "conv": 6, "cq": 1,
    "gates": 1, "beta": 1, "gsq": 1, "sp_dt": 1, "gdn_sum": 1, "gdn_rn": 1, "gcum": 1, "Gb_mm": 1, "Gb": 2,
    "eG": 1, "bb_mm": 1, "Gc_mm": 1, "Gc": 1, "gq": 1, "kq": 1, "kq_q": 1, "vb": 1, "Gdiff": 1, "E": 1, "Glast": 1,
    "eGd": 1, "kd": 1, "EM": 4, "KQ_mm": 1, "KQ": 3, "gdn_rows_mm": 2, "gdn_rows": 1, "gc_kept": 1,
    "gla_z": 1, "gla_ab": 1, "gla_q": 1, "gla_min": 1, "gla_ln": 1, "At_zero": 1, "lD": 6, "lE": 6, "lqs": 6,
    "lks": 6, "gla_lev": 7, "gla_take": 14, "lBl": 1, "leB": 1, "lkd": 1, "gla_rows_mm": 2, "gla_rows": 1,
    "xc": 2, "rg_mm": 1, "rg_gates": 4, "sp_lam": 1, "rg_y": 2, "rg_a": 1, "rg_b2": 1, "rg_b": 1, "rg_h": 2,
    "rg_kept": 1, "rgc_kept": 1, "lS_mm": 1, "lS": 4, "o_ready": 4, "o_hi": 4, "o_lo": 4, "LB": 12, "T_mm": 10,
    "YNY_mm": 10, "X": 10, "Y": 12, "T": 10, "R0_mm": 2, "R0T": 2, "rR_mm": 5, "gR_mm": 5, "rR": 5,
    "gR": 5, "rU_mm": 5, "gU_mm": 5, "rU": 5, "gU": 5, "rM_mm": 4, "gM_mm": 4, "rM": 8, "gM": 8, "out_mm": 3,
    "yo": 3, "yo_dec": 3, "ysq": 3, "yrs": 3, "yo_done": 3, "mean_mm": 1, "mean_read": 1, "var_mm": 3, "VM": 6, "dec_mm": 3,
    "dec_decay": 3, "dec_add": 3,
}
V_STEPS, A_STEPS, G_STEPS = 111, 35, 17


class Signal:

    def __init__(self, ctx, nc, name, n=1):
        self.sem, self.n, self.given, self.name = ctx.enter_context(nc.semaphore(name)), n, 0, name

    def upto(self, layer, k=None):
        return layer * self.n + (self.n if k is None else k)


class Steps:

    def __init__(self, eng, own, layer, wait):
        self.eng, self.own, self.layer, self.last, self.wait = eng, own, layer, None, wait

    def __call__(self, ins, sig=None):
        sig = sig or self.own
        ins.then_inc(sig.sem, 1)
        sig.given += 1
        self.last = (sig, sig.given)
        return ins

    def settle(self):
        sig, k = self.last
        self.wait(self.eng, sig, sig.upto(self.layer, k))


def program(nc, xT, wts, par, cst, sin, mst, yT, sout, mout):
    with ExitStack() as ctx:
        def sb(name, shape, dt=F32):
            return ctx.enter_context(nc.sbuf_tensor(name, shape, dt))

        def signal(name, n=1):
            s = Signal(ctx, nc, name, n)
            signals.append(s)
            return s

        signals = []
        x = sb("x", [128, KT, TOK])
        xh = sb("xh", [128, KT, TOK], F32R)
        xl = sb("xl", [128, KT, TOK], F32R)
        raw = sb("raw", [128, RING, 1024])
        wh = sb("wh", [128, RING, 1024], F32R)
        wl = sb("wl", [128, RING, 1024], F32R)
        pr = sb("pr", [128, PARN])
        cs = sb("cs", [128, CSTN])
        si = sb("si", [128, SINN])
        so = sb("so", [128, SOUTN])
        ms = sb("ms", [128, MSTN])
        chain = sb("chain", [128, 2 * 4 * 128 + 4 * 64])
        rstd = sb("rstd", [128, TOK])
        lnt = sb("lnt", [128, TOK])
        tiny = sb("tiny", [128, 16])
        with nc.sbuf_tensor("hid_h", [128, FT, TOK], F32R) as hid_h, \
                nc.sbuf_tensor("hid_l", [128, FT, TOK], F32R) as hid_l, \
                nc.sbuf_tensor("gus", [128, 4, TOK], F32) as gus:
            pass
        ar = sb("ar", [128, 80 * TOK])
        ps = ctx.enter_context(nc.psum_tensor("ps", [128, 8, 512], F32))

        def A(u, n, pat=None, **kw):
            v = ar[:, u * TOK:u * TOK + n]
            return v.rearrange(pat, **kw) if pat else v

        def P(name, i=0, n=1):
            return pr[:, PAR[name][0] + i:PAR[name][0] + i + n]

        def C(name, i=0, n=None):
            at, w = CST[name]
            return cs[:, at + i:at + i + (w if n is None else n)]

        PT = "q (p t) -> q p t"
        CP = "q (c p t) -> q c p t"
        rw_g, rw_bonus, rP = (A(u, 640, PT, p=2) for u in (0, 2, 4))
        kkr = A(6, 1280, "q (c p k t) -> q c p k t", c=NC, p=2, k=2)
        BE = A(10, 1280, "q (c p k t) -> q c p k t", c=NC, p=2, k=2)
        CD = A(14, 1280, "q (c p k t) -> q c p k t", c=NC, p=2, k=2)
        rVt, kLt, bLt = (A(u, 640, CP, c=NC, p=2) for u in (18, 20, 22))
        gz, eG, kbe, qe = (A(u, 640, PT, p=2) for u in (24, 26, 28, 30))
        KQ = A(32, 1280, "q (c p k t) -> q c p k t", c=NC, p=2, k=2)
        bvt, gkdt = (A(u, 640, CP, c=NC, p=2) for u in (36, 38))
        gt = A(40, 640, PT, p=2)
        small = A(42, 320)
        gla = A(43, 1280, "q (k t) -> q k t", k=4)
        rgp = A(47, 2 * CVP, PT, p=2)
        rgg = A(50, 640, PT, p=2)
        rwp = A(52, 7 * RWP, PT, p=7)
        xm = A(60, 7 * TOK, PT, p=7)
        sg, cum, Pinv = (A(u, 640, PT, p=2) for u in (67, 69, 71))
        Pprev, kmod, bPi, kPi, bL, kL, kk = (A(u, 640, PT, p=2) for u in (26, 28, 30, 32, 34, 36, 38))
        ra, rsq, rtm = (A(u, 640, PT, p=2) for u in (52, 54, 56))
        gcp = A(73, 6 * CVP, PT, p=6)
        cq = A(52, 6 * TOK, PT, p=6)
        gsq = A(58, 4 * TOK, PT, p=4)
        Gb, Gd, kd, vb = (A(u, 640, PT, p=2) for u in (62, 78, 74, 76))
        E = A(64, 640, CP, c=NC, p=2)
        EM = A(66, 1280, "q (c p k t) -> q c p k t", c=NC, p=2, k=2)
        kq = A(70, 1280, "q (c p k t) -> q c p k t", c=NC, p=2, k=2)
        Gc = tiny[:, 0:10].rearrange("q (c p) -> q c p", c=NC)
        At = A(72, 640, "q (p c t) -> q p c t", p=2, c=NC)
        lqe = A(74, 320)
        lVt = A(75, 640, CP, c=NC, p=2)
        lkt = A(77, 320, "q (c p t) -> q c p t", c=NC, p=2)
        lB, lE, lkd, ltm = (A(u, 320) for u in (78, 61, 66, 67))
        lqs, lks = [A(62, 320), A(63, 320)], [A(64, 320), A(65, 320)]
        xc, rr, ri, rga, rgb, rgt = (A(u, 640, PT, p=2) for u in (52, 54, 56, 58, 68, 70))
        X, Y, Tm = (A(u, 1280, "q (m s) -> q m s", m=20) for u in (52, 56, 60))
        LB = [A(64 + 4 * i, 1280, "q (m s) -> q m s", m=20) for i in range(2)]
        RR = [A(u, 640, CP, c=NC, p=2) for u in (52, 60)]
        UU = [A(u, 640, CP, c=NC, p=2) for u in (54, 62)]
        VM = A(64, 1024, "q (p s v) -> q p s v", p=2, s=DECB)
        UM = A(68, 1024, "q (p s v) -> q p s v", p=2, s=DECB)
        yo, yc, ysq = (A(u, 640, PT, p=2) for u in (43, 45, 47))
        R0T = [A(51, 256, "q (g p t) -> q g p t", g=2, p=2)[:, g] for g in range(2)]
        nsq = A(49, 8 * TOK, PT, p=8)

        def mstate(name, p=2):
            at, n = MST[name]
            return ms[:, at:at + n].rearrange("q (p s v) -> q p s v", p=p, s=NSEQ)

        Mrw, Mgdn = mstate("rw"), mstate("gdn")
        Mgla = mstate("gla", 1)[:, 0]
        chain_of = [chain[:, 512 * i:512 * i + 512].rearrange("q (c p v) -> q c p v", c=4, p=2) for i in range(2)]
        chain_l = chain[:, 1024:1280].rearrange("q (c v) -> q c v", c=4)

        def io(t, spec, name, pat, **kw):
            at, n = spec[name]
            return t[:, at:at + n].rearrange(pat, **kw)

        tri = C("tri").rearrange("q (d k t) -> q d k t", d=2, k=2)
        lev = C("lev").rearrange("q (l t) -> q l t", l=7)
        sel = P("glag", 0, 256).rearrange("q (p m) -> q p m", p=2)
        wrg = [P("wa", 0, 128).rearrange("q (p m) -> q p m", p=2), P("wx", 0, 128).rearrange("q (p m) -> q p m", p=2)]

        half = [slice(0, 64), slice(64, 128)]
        I64 = [lev[half[b], 0, :] for b in range(2)]

        def seqs(v, pad, first=0, n=DECT):
            at = (pad + SEQ) if pad else SEQ
            flat = v[..., at:at + DECB * (DECT + pad)]
            if len(v.shape) == 2:
                return flat.rearrange("q (s t) -> q s t", s=DECB)[:, :, first:first + n]
            return flat.rearrange("q p (s t) -> q p s t", s=DECB)[:, :, :, first:first + n]

        def chunked(v):
            return v.rearrange("q p (c t) -> q c p t", c=NC)

        def splits(layer, first, count, split, eng):
            with eng.Fori(0, count // RING) as i:
                for k in range(RING):
                    split(layer, first + k, i)
            for k in range(count // RING * RING, count):
                split(layer, first + k)

        def banks(bank, runs, w=64):
            lo, hi = runs
            flat = ps[:, bank:bank + 3, :].rearrange("q b t -> q (b t)") if bank <= 5 else \
                ps[:, bank:8, :].rearrange("q b t -> q (b t)")
            return flat[:, lo * w:hi * w].rearrange("q (u t) -> q u t", u=hi - lo)

        def blocks(level):
            return 10 if level <= 2 else 8

        raw_in = [signal(f"raw_in{s}") for s in range(RING)]
        const_in, y_out = signal("const_in"), signal("y_out")
        par_in, state_in, state_out = (signal(n) for n in ("par_in", "state_in", "state_out"))
        hi_ready, lo_ready = signal("hi_ready", UNITS), signal("lo_ready", UNITS)
        unit_used = signal("unit_used", UNITS)
        v_step, a_step, g_step = signal("v_step", V_STEPS), signal("a_step", A_STEPS), signal("g_step", G_STEPS)
        sq_ready, xh_ready, xl_ready, x_new = (signal(n, 24) for n in ("sq_ready", "xh_ready", "xl_ready", "x_new"))
        sum_mm, rstd_ready = signal("sum_mm", 3), signal("rstd_ready", 3)
        gs_ready, gu_read, sil_ready, act_ready, hh_ready, hl_ready = (
            signal(n, 2 * FT) for n in ("gs_ready", "gu_read", "sil_ready", "act_ready", "hh_ready", "hl_ready"))
        in_read = signal("in_read", IN_TILES)
        S = {name: signal(name, n) for name, n in MIX_SIGNALS.items()}

        passed = signal("passed")
        OWN_WAITS = (mybir.EngineType.PE, mybir.EngineType.Pool)

        def apart(eng, s, value):
            eng.wait_ge(s.sem, value).then_inc(passed.sem, 1)

        def plain(eng, s, value):
            eng.wait_ge(s.sem, value)

        def on(eng, layer, s, k=None):
            s = S[s] if isinstance(s, str) else s
            apart(eng, s, s.upto(layer, k)) if eng.engine in OWN_WAITS else eng.wait_ge(s.sem, s.upto(layer, k))

        def per_slot(s):
            return len(range(s, UNITS, RING))

        def raw_landed(eng, layer, n, i):
            s = n % RING
            eng.wait_ge(raw_in[s].sem, (layer * per_slot(s) + i + n // RING + 1) * 16)

        def slot_free(eng, layer, n, i):
            if n >= RING:
                eng.wait_ge(unit_used.sem, layer * UNITS + i * RING + n - RING + 1)

        block = ctx.enter_context(nc.Block())

        @block.sync
        def _(sp):
            sp.dma_start(cs[:], cst).then_inc(const_in.sem, 16)
            sp.dma_start(x[:], xT).then_inc(const_in.sem, 16)

            def load(layer, n, i=0):
                s = n % RING
                unit = layer * UNITS + i * RING + n
                sp.dma_start(raw[:, s, :], wts[bass.ds(unit, 1), :, :].rearrange("n p c -> (n p) c")) \
                    .then_inc(raw_in[s].sem, 16)

            with sp.Fori(0, DEPTH) as layer:
                for n in range(RING):
                    load(layer, n)
                with sp.Fori(0, UNITS // RING - 1) as i:
                    for n in range(RING, 2 * RING):
                        sp.wait_ge(lo_ready.sem, layer * UNITS + i * RING + n - RING + 1)
                        load(layer, n, i)
                for n in range(UNITS // RING * RING, UNITS):
                    sp.wait_ge(lo_ready.sem, layer * UNITS + n - RING + 1)
                    load(layer, n)
                apart(sp, lo_ready, layer * UNITS + UNITS)
            sp.wait_ge(x_new.sem, DEPTH * 24 + KT)
            sp.dma_start(yT, x[:]).then_inc(y_out.sem, 16)
            sp.wait_ge(y_out.sem, 16)

        @block.tensor
        def _(pe):
            def put(ins, name):
                ins.then_inc(S[name].sem, 1)
                S[name].given += 1

            def three(out, a, b, rh, rl, start, stop):
                pe.matmul(out, a, rh, start=start, stop=False)
                pe.matmul(out, a, rl, start=False, stop=False)
                return pe.matmul(out, b, rh, start=False, stop=stop)

            def wsl(s, k):
                return wh[:, s, k * 128:(k + 1) * 128], wl[:, s, k * 128:(k + 1) * 128]

            def tile_mm(layer, n, bank, i=0):
                pe.wait_ge(lo_ready.sem, layer * UNITS + i * RING + n + 1)
                for k in range(KT):
                    ins = three(ps[:, bank, 0:TOK], *wsl(n % RING, k), xh[:, k, :], xl[:, k, :], k == 0, k == KT - 1)
                ins.then_inc(unit_used.sem, 1)

            def norm_sums(layer, which):
                for k in range(KT):
                    pe.wait_ge(sq_ready.sem, layer * 24 + which * KT + k + 1)
                    ins = pe.matmul(ps[:, 7, 0:TOK], C("ones"), nsq[:, k, :], start=(k == 0), stop=(k == KT - 1))
                ins.then_inc(sum_mm.sem, 1)

            def ffn(layer, f):
                base = f * FFN2
                on(pe, layer, xl_ready, 2 * f * KT + KT)

                def gate_up(i, m):
                    tile_mm(layer, base + 2 * m, 2 * m, i)
                    tile_mm(layer, base + 2 * m + 1, 2 * m + 1, i)

                gate_up(0, 0)
                norm_sums(layer, 2 * f)
                gate_up(0, 1)
                with pe.Fori(1, FT // 2) as i:
                    for m in range(2):
                        pe.wait_ge(gu_read.sem, layer * 2 * FT + f * FT + i * 2 + m - 1)
                        gate_up(i, m)
                on(pe, layer, hl_ready, (f + 1) * FT)

                def down(k, i=0, start=False, stop=False):
                    n = base + 2 * FT + k
                    pe.wait_ge(lo_ready.sem, layer * UNITS + i * RING + n + 1)
                    at = bass.ds(i * RING + k, 1)
                    rh = hid_h[:, at, :].rearrange("q a t -> q (a t)")
                    rl = hid_l[:, at, :].rearrange("q a t -> q (a t)")
                    for m in range(KT):
                        ins = three(ps[:, m, 0:TOK], *wsl(n % RING, m), rh, rl, start, stop)
                    ins.then_inc(unit_used.sem, 1)

                down(0, start=True)
                with pe.Fori(0, (FT - 2) // RING) as i:
                    for k in range(1, 1 + RING):
                        down(k, i)
                down(FT - 1, stop=True)

            def each(fn, chunks=range(NC)):
                for c in chunks:
                    for p in range(2):
                        for b in range(2):
                            ins = fn(c, p, b)
                return ins

            def cht(v, c, p, b):
                return v[half[b], p, c * CH:(c + 1) * CH]

            def lora(layer):
                on(pe, layer, "lora_in")
                lo = P("lora", 0, 256)
                for rows, bank in ((slice(0, 32), 2), (slice(32, 64), 4), (slice(64, 128), 6)):
                    for p in range(2):
                        ins = pe.matmul(ps[:, bank + p, 0:TOK], lo[rows, p * 128:p * 128 + 128], xm[rows, 6, :], start=True, stop=True)
                    put(ins, "lora_mm")

            def rw_sums(layer):
                on(pe, layer, "sg")
                on(pe, layer, "kk_sq")
                for p in range(2):
                    ins = pe.matmul(ps[:, 2 + p, 0:TOK], C("hones"), rsq[:, p, :], start=True, stop=True)
                put(ins, "kk_sum")
                on(pe, layer, "ra")
                on(pe, layer, "rkr")
                for p in range(2):
                    ins = pe.matmul(ps[:, 4 + p, 0:TOK], C("hones"), rtm[:, p, :], start=True, stop=True)
                put(ins, "rk_sum")

            def products(src, rhs, three_banks, name):
                def f(c, p, b):
                    return pe.matmul(ps[half[b], three_banks[c // 2], ((c % 2) * 2 + p) * 128:][:, 0:128],
                                     cht(src, c, p, b), rhs[half[b], c, p].rearrange("q k t -> q (k t)"),
                                     start=True, stop=True)
                put(each(f), name)

            def rw_products(layer):
                on(pe, layer, "rw_ops")
                on(pe, layer, "bPi")
                on(pe, layer, "kPi")
                on(pe, layer, "rw_gc")
                on(pe, layer, "bonus")
                on(pe, layer, "kk_rn")
                products(bPi, kkr, (2, 3, 6), "rw_pairs")
                products(kPi, kkr, (4, 5, 7), "rw_pairs")

            def to_rows(src, bank, name):
                def f(c, p, b):
                    u = c * 2 + p
                    return pe.matmul(ps[half[b], bank + u // 8, (u % 8) * 64:(u % 8) * 64 + 64], cht(src, c, p, b), I64[b],
                                     start=True, stop=True)
                put(each(f), name)

            def rw_rows(layer):
                on(pe, layer, "rw_pairs_read")
                on(pe, layer, "kbL")
                to_rows(xm[:, 4:6], 2, "rw_rows_mm")
                to_rows(kL, 4, "rw_rows_mm")
                to_rows(bL, 6, "rw_rows_mm")

            def gdn_sums(layer):
                on(pe, layer, "gsq")
                on(pe, layer, "rw_rows")
                for k in range(4):
                    ins = pe.matmul(ps[:, 2 + k, 0:TOK], C("hones"), gsq[:, k, :], start=True, stop=True)
                put(ins, "gdn_sum")

            def gdn_bcast(layer):
                on(pe, layer, "gcum")
                R = slice(32, 32 + NH)
                for p in range(2):
                    ins = pe.matmul(ps[:, 6 + p, 0:TOK], sel[R, p, :], small[R, :], start=True, stop=True)
                put(ins, "Gb_mm")
                on(pe, layer, "gdn_rn")
                on(pe, layer, "beta")
                for p in range(2):
                    ins = pe.matmul(ps[:, 2 + p, 0:TOK], sel[0:NH, p, :], small[0:NH, :], start=True, stop=True)
                put(ins, "bb_mm")
                on(pe, layer, "Gb")
                def f(c, p, b):
                    return pe.matmul(ps[half[b], 4, c * 2 + p:c * 2 + p + 1], cht(Gb, c, p, b), I64[b][:, 0:1], start=True, stop=True)
                put(each(f), "Gc_mm")

            def gdn_products(layer):
                on(pe, layer, "kq")
                on(pe, layer, "kq_q")
                on(pe, layer, "Gb")
                products(cq[:, 2:4], kq, (5, 6, 7), "KQ_mm")

            def gdn_rows(layer):
                on(pe, layer, "vb")
                to_rows(vb, 2, "gdn_rows_mm")
                on(pe, layer, "kd")
                on(pe, layer, "KQ")
                on(pe, layer, "Gc")
                to_rows(kd, 4, "gdn_rows_mm")

            def gla_gate(layer):
                on(pe, layer, "KQ")
                ins = pe.matmul(ps[:, 7, 0:TOK], P("glag", 0, 128)[64:80, :], small[64:80, :], start=True, stop=True)
                put(ins, "gla_z")

            def gla_levels(layer):
                on(pe, layer, "gdn_rows")
                on(pe, layer, "gla_q")
                for l in range(7):
                    if l:
                        on(pe, layer, "lqs", l)
                        on(pe, layer, "lks", l)
                    if l >= 2:
                        on(pe, layer, "gla_take", 2 * (l - 1))
                    kk_, qq_ = (gla[:, 1, :], gla[:, 0, :]) if l == 0 else (lks[l % 2], lqs[l % 2])
                    for c in range(NC if l <= 3 else DEC):
                        for h in range(NH):
                            r = slice(DK * h, DK * h + DK)
                            t = slice(c * CH, (c + 1) * CH)
                            ins = pe.matmul(ps[half[h % 2], 2 + 2 * (l % 2) + h // 2, t], kk_[r, t], qq_[r, t], start=True, stop=True)
                    put(ins, "gla_lev")

            def gla_rows(layer):
                on(pe, layer, "lkd")
                on(pe, layer, "gla_take")
                on(pe, layer, "gla_ab")
                on(pe, layer, "gla_min")
                for c in range(NC):
                    for h in range(NH):
                        r = slice(DK * h, DK * h + DK)
                        ins = pe.matmul(ps[half[h % 2], 6 + h // 2, c * DK:c * DK + DK],
                                        lkd[r, c * CH:(c + 1) * CH], lev[r, 0, DK * (h % 2):DK * (h % 2) + DK], start=True, stop=True)
                put(ins, "gla_rows_mm")
                to_rows(gla[:, 2:4], 2, "gla_rows_mm")

            def gla_states(layer):
                on(pe, layer, "gla_rows")
                on(pe, layer, "rg_gates")
                for h in range(NH):
                    b, p, r = h % 2, h // 2, slice(DK * h, DK * h + DK)
                    for c in range(DEC):
                        ins = pe.matmul(ps[r, 6, c * 64:c * 64 + 64], lkt[half[b], c, p, :], lVt[half[b], c, p, :], start=True, stop=True)
                put(ins, "lS_mm")

            def rg_gates(layer):
                on(pe, layer, "xc")
                on(pe, layer, "gla_rows")
                for g in range(2):
                    for p in range(2):
                        for b in range(2):
                            ins = pe.matmul(ps[half[b], 4 + 2 * g + p, 0:TOK], wrg[g][half[b], p, :], xc[half[b], p, :],
                                            start=True, stop=True)
                put(ins, "rg_mm")

            def inverse(layer):
                on(pe, layer, "rg_gates")
                on(pe, layer, "lS")
                for l in range(1, 6):
                    n = blocks(l)

                    def unit(bank, g, m, b):
                        return ps[half[b], bank + 2 * g + m // 8, (m % 8) * 64:(m % 8) * 64 + 64]

                    for g in range(2):
                        on(pe, layer, "LB", 2 * l + g + 1)
                        on(pe, layer, "X", 2 * (l - 1) + g + 1)
                        for m in range(n):
                            for b in range(2):
                                ins = pe.matmul(unit(0, g, m, b), LB[l % 2][half[b], 10 * g + m], X[half[b], 10 * g + m],
                                                start=True, stop=True)
                        put(ins, "T_mm")
                    for g in range(2):
                        on(pe, layer, "T", 2 * (l - 1) + g + 1)
                        for m in range(n):
                            for b in range(2):
                                ins = pe.matmul(unit(4, g, m, b), Tm[half[b], 10 * g + m], Y[half[b], 10 * g + m],
                                                start=True, stop=True)
                        put(ins, "YNY_mm")

            def recurrences(layer):
                on(pe, layer, "Y")
                on(pe, layer, "T")
                apart(pe, state_in, layer * 32 + 32)
                for g, M in enumerate((Mrw, Mgdn)):
                    for p in range(2):
                        for b in range(2):
                            for q in range(DECB):
                                t = slice(q * 8, q * 8 + 8)
                                rhs = kkr[half[b], DEC, p, 0, t] if g == 0 else kbe[half[b], p, SEQ:][:, t]
                                ins = pe.matmul(ps[half[b], 4 + g, p * 64 + q * 8:p * 64 + q * 8 + 8], M[half[b], p, 1 + q, :],
                                                rhs, start=True, stop=True)
                    put(ins, "R0_mm")
                on(pe, layer, "chain_zero")
                for c in range(NC):
                    for g in range(2):
                        if c == DEC:
                            on(pe, layer, "R0T", g + 1)
                        if c:
                            on(pe, layer, ("rM", "gM")[g], 2 * min(c, DEC))
                            on(pe, layer, ("rR", "gR")[g], c)
                        for p in range(2):
                            for b in range(2):
                                o = ps[half[b], g, p * 64:p * 64 + 64]
                                if c == DEC:
                                    a_, r_ = R0T[g][half[b], p, :], I64[b]
                                else:
                                    a_, r_ = (kkr[half[b], c, p, 0, :] if g == 0 else cht(kbe, c, p, b)), chain_of[g][half[b], c, p, :]
                                ins = pe.matmul(o, a_, r_, start=True, stop=(g == 1))
                                if g == 0:
                                    ins = pe.matmul(o, CD[half[b], c, p, 0, :], rVt[half[b], c, p, :], start=False, stop=True)
                        put(ins, ("rR_mm", "gR_mm")[g])
                    for g in range(2):
                        on(pe, layer, ("rR", "gR")[g], c + 1)
                        for p in range(2):
                            for b in range(2):
                                ins = pe.matmul(ps[half[b], 2 + g, p * 64:p * 64 + 64], Y[half[b], g * 10 + c * 2 + p],
                                                RR[g][half[b], c, p, :], start=True, stop=True)
                        put(ins, ("rU_mm", "gU_mm")[g])
                    if c == DEC:
                        break
                    for g in range(2):
                        on(pe, layer, ("rU", "gU")[g], c + 1)
                        for p in range(2):
                            for b in range(2):
                                o = ps[half[b], 6 + g, p * 64:p * 64 + 64]
                                if g == 0:
                                    pe.matmul(o, kLt[half[b], c, p, :], rVt[half[b], c, p, :], start=True, stop=False)
                                    ins = pe.matmul(o, bLt[half[b], c, p, :], UU[0][half[b], c, p, :], start=False, stop=True)
                                else:
                                    ins = pe.matmul(o, gkdt[half[b], c, p, :], UU[1][half[b], c, p, :], start=True, stop=True)
                        put(ins, ("rM_mm", "gM_mm")[g])

            def output(layer, g):
                if g == 0:
                    on(pe, layer, "rU")
                    on(pe, layer, "gU")
                    on(pe, layer, "rM")
                    on(pe, layer, "gM")
                if g == 2:
                    on(pe, layer, "lS")
                    on(pe, layer, "mean_read")
                def f(c, p, b):
                    h = 2 * p + b
                    r = slice(DK * h, DK * h + DK)
                    o = ps[half[b], 2 * g + p, c * CH:(c + 1) * CH]
                    if g == 0:
                        rhs = kkr[half[b], c, p, 1, :]
                        terms = [(rVt[half[b], c, p, :], CD[half[b], c, p, 1, :]), (UU[0][half[b], c, p, :], BE[half[b], c, p, 1, :])]
                    elif g == 1:
                        rhs = cht(qe, c, p, b)
                        terms = [(UU[1][half[b], c, p, :], KQ[half[b], c, p, 1, :])]
                    else:
                        rhs = lqe[r, c * CH:(c + 1) * CH]
                        terms = [(lVt[half[b], c, p, :], At[half[b], p, c, :])]
                    if c < DEC:
                        pe.matmul(o, chain_of[g][half[b], c, p, :] if g < 2 else chain_l[r, c, :], rhs, start=True, stop=False)
                    else:
                        for q in range(DECB):
                            t = slice(q * DECT, (q + 1) * DECT)
                            pe.matmul(ps[half[b], 2 * g + p, TOK + q * DECT:TOK + (q + 1) * DECT],
                                      (Mrw, Mgdn)[g][half[b], p, 1 + q, :] if g < 2 else Mgla[r, 1 + q, :], rhs[:, t],
                                      start=True, stop=True)
                    for i, (l_, r_) in enumerate(terms):
                        ins = pe.matmul(o, l_, r_, start=(c == DEC and i == 0), stop=(i == len(terms) - 1))
                    return ins
                put(each(f), "out_mm")

            def head_sums(layer, g):
                if g == 0:
                    on(pe, layer, "yo_dec", 1)
                    for p in range(2):
                        ins = pe.matmul(ps[:, 4 + p, 0:TOK], C("hones"), yo[:, p, :], start=True, stop=True)
                    put(ins, "mean_mm")
                on(pe, layer, "ysq", g + 1)
                if g:
                    on(pe, layer, "yrs", g)
                for p in range(2):
                    ins = pe.matmul(ps[:, 6 + p, 0:TOK], C("hones"), ysq[:, p, :], start=True, stop=True)
                put(ins, "var_mm")

            def dec_states(layer, g):
                on(pe, layer, "VM", 2 * (g + 1))
                on(pe, layer, "yo_dec", 2)
                if g == 2:
                    on(pe, layer, "dec_add", 1)
                b0 = 2 * (g % 2)
                for p in range(2):
                    for b in range(2):
                        h = 2 * p + b
                        r = slice(DK * h, DK * h + DK)
                        vm = VM[half[b], p].rearrange("q s v -> q (s v)")
                        um = UM[half[b], p].rearrange("q s v -> q (s v)")
                        o = ps[half[b], b0 + p, :]
                        if g == 0:
                            pe.matmul(o, kLt[half[b], DEC, p, :], vm, start=True, stop=False)
                            ins = pe.matmul(o, bLt[half[b], DEC, p, :], um, start=False, stop=True)
                        elif g == 1:
                            ins = pe.matmul(o, gkdt[half[b], DEC, p, :], um, start=True, stop=True)
                        else:
                            ins = pe.matmul(ps[r, b0, :], lkt[half[b], DEC, p, :], vm, start=True, stop=True)
                put(ins, "dec_mm")

            after_tile = {11: [lora], 15: [rw_sums], 19: [rw_products], 22: [rw_rows]}
            pe.wait_ge(const_in.sem, 32)
            with pe.Fori(0, DEPTH) as layer:
                ffn(layer, 0)
                on(pe, layer, xl_ready, 2 * KT)
                for m in range(IN_TILES):
                    if m >= 2:
                        on(pe, layer, in_read, m - 1)
                    tile_mm(layer, IN0 + m, m % 2)
                    if m == 0:
                        norm_sums(layer, 1)
                    for stage in after_tile.get(m, []):
                        stage(layer)
                for stage in (gdn_sums, gdn_bcast, gdn_products, gdn_rows, gla_gate, gla_levels, gla_rows,
                              rg_gates, gla_states, inverse, recurrences):
                    stage(layer)
                output(layer, 0)
                head_sums(layer, 0)
                output(layer, 1)
                dec_states(layer, 0)
                head_sums(layer, 1)
                output(layer, 2)
                dec_states(layer, 1)
                head_sums(layer, 2)
                dec_states(layer, 2)
                on(pe, layer, "o_lo", 4)
                on(pe, layer, "dec_add")
                for m in range(KT):
                    tile_mm(layer, OUT0 + m, m)
                ffn(layer, 1)
            for k in range(KT):
                pe.wait_ge(sq_ready.sem, DEPTH * 24 + k + 1)
                ins = pe.matmul(ps[:, 7, 0:TOK], C("ones"), nsq[:, k, :], start=(k == 0), stop=(k == KT - 1))
            ins.then_inc(sum_mm.sem, 1)

        @block.scalar
        def _(act):
            def split_hi(layer, n, i=0):
                raw_landed(act, layer, n, i)
                slot_free(act, layer, n, i)
                act.activation(wh[:, n % RING, :], raw[:, n % RING, :], ACT.Copy).then_inc(hi_ready.sem, 1)

            def norm_split(layer, which, name):
                for k in range(KT):
                    if which:
                        act.wait_ge(x_new.sem, layer * 24 + (which - 1) * KT + k + 1)
                    act.activation(nsq[:, k, :], x[:, k, :], ACT.Square).then_inc(sq_ready.sem, 1)
                    act.activation(xh[:, k, :], x[:, k, :], ACT.Copy, scale=P(name, k)).then_inc(xh_ready.sem, 1)

            def rms(layer, which):
                act.wait_ge(sum_mm.sem, layer * 3 + which + 1)
                st(act.activation(lnt[:], ps[:, 7, 0:TOK], ACT.Ln, bias=C("e6"), scale=1.0 / D))
                st.settle()
                act.activation(rstd[:], lnt[:], ACT.Exp, scale=-0.5).then_inc(rstd_ready.sem, 1)

            def ffn(layer, f):
                base = f * FFN2

                def gate(m, i):
                    t = layer * 2 * FT + f * FT + i * 2 + m
                    split_hi(layer, base + RING + 2 * m, i)
                    act.wait_ge(gs_ready.sem, t + 1)
                    act.activation(gus[:, m, :], gus[:, m, :], ACT.Silu).then_inc(sil_ready.sem, 1)
                    split_hi(layer, base + RING + 2 * m + 1, i)
                    act.wait_ge(act_ready.sem, t + 1)
                    at = bass.ds(i * 2 + m, 1)
                    act.activation(hid_h[:, at, :].rearrange("q a t -> q (a t)"), gus[:, m, :], ACT.Copy).then_inc(hh_ready.sem, 1)

                with act.Fori(0, FT // 2) as i:
                    for m in range(2):
                        gate(m, i)
                splits(layer, base + 2 * FT + RING, min(FT, UNITS - RING - base - 2 * FT), split_hi, act)

            with act.Fori(0, DEPTH) as layer:
                st = Steps(act, a_step, layer, plain)

                def say(ins, name):
                    return st(ins, S[name])

                def fetch(dst, src, sem):
                    act.dma_start(dst, src[bass.ds(layer, 1), :, :].rearrange("a q n -> (a q) n")).then_inc(sem.sem, 16)

                fetch(pr[:], par, par_in)
                fetch(si[:], sin, state_in)
                fetch(ms[:], mst, state_in)
                for n in range(RING):
                    split_hi(layer, n)
                act.wait_ge(const_in.sem, 32)
                act.wait_ge(par_in.sem, layer * 16 + 16)
                norm_split(layer, 0, "n1")
                rms(layer, 0)
                ffn(layer, 0)
                norm_split(layer, 1, "nm")
                rms(layer, 1)
                for m in range(9):
                    split_hi(layer, IN0 + RING + m)
                on(act, layer, "xm")
                st(act.activation(xm[0:32, 6, :], xm[0:32, 6, :], ACT.Tanh))
                say(act.activation(xm[64:128, 6, :], xm[64:128, 6, :], ACT.Sigmoid), "lora_in")
                for m in range(9, 13):
                    split_hi(layer, IN0 + RING + m)
                on(act, layer, "lora_mm", 1)
                for p in range(2):
                    say(act.activation(sg[:, p, :], ps[:, 2 + p, 0:TOK], ACT.Sigmoid, bias=P("w0", p)), "sg")
                on(act, layer, "lora_mm", 2)
                on(act, layer, "shift_kept")
                for p in range(2):
                    say(act.activation(ra[:, p, :], ps[:, 4 + p, 0:TOK], ACT.Sigmoid, bias=P("a0", p)), "ra")
                on(act, layer, "lora_mm", 3)
                for p in range(2):
                    say(act.activation(rw_g[:, p, :], ps[:, 6 + p, 0:TOK], ACT.Copy), "rw_gc")
                for m in range(13, 17):
                    split_hi(layer, IN0 + RING + m)
                on(act, layer, "cum")
                st(act.activation(rP[:], cum[:], ACT.Exp, scale=-WDEC))
                st(act.activation(Pinv[:], cum[:], ACT.Exp, scale=WDEC))
                on(act, layer, "prev")
                say(act.activation(Pprev[:], sg[:], ACT.Exp, scale=-WDEC), "rw_P")
                on(act, layer, "kk_sum")
                for p in range(2):
                    st(act.activation(rsq[:, p, :], ps[:, 2 + p, 0:TOK], ACT.Ln, bias=C("e12")))
                st.settle()
                say(act.activation(rsq[:], rsq[:], ACT.Exp, scale=-0.5), "kk_rn")
                for m in range(17, 22):
                    split_hi(layer, IN0 + RING + m)
                on(act, layer, "rw_rows_mm", 1)
                st(act.activation(rVt[:].rearrange("q c p t -> q (c p) t"), banks(2, (0, 10)), ACT.Copy))
                on(act, layer, "rw_rows_mm", 2)
                st(act.activation(kLt[:].rearrange("q c p t -> q (c p) t"), banks(4, (0, 10)), ACT.Copy))
                on(act, layer, "rw_rows_mm", 3)
                say(act.activation(bLt[:].rearrange("q c p t -> q (c p) t"), banks(6, (0, 10)), ACT.Copy), "rw_rows")
                for m in range(22, 26):
                    split_hi(layer, IN0 + RING + m)
                on(act, layer, "conv")
                say(act.activation(cq[:], cq[:], ACT.Silu), "cq")
                on(act, layer, in_read)
                st(act.activation(gz[:], gz[:], ACT.Silu))
                st(act.activation(gt[:], gt[:], ACT.Silu))
                say(act.activation(rgg[:], rgg[:], ACT.Gelu_apprx_tanh), "gates")
                R = slice(32, 32 + NH)
                say(act.activation(small[0:NH, :], small[0:NH, :], ACT.Sigmoid), "beta")
                on(act, layer, "cq")
                say(act.activation(gsq[:], cq[:, 0:4, :], ACT.Square), "gsq")
                st(act.activation(tiny[R, 10:11], P("alog")[R], ACT.Exp))
                st(act.activation(lnt[R, :], small[R, :], ACT.Abs, bias=P("dtb")[R]))
                st.settle()
                st(act.activation(lnt[R, :], lnt[R, :], ACT.Exp, scale=-1.0))
                st.settle()
                say(act.activation(lnt[R, :], lnt[R, :], ACT.Ln, bias=C("one")[R]), "sp_dt")
                on(act, layer, "gdn_sum")
                for k in range(4):
                    st(act.activation(gsq[:, k, :], ps[:, 2 + k, 0:TOK], ACT.Ln, bias=C("e12")))
                st.settle()
                say(act.activation(gsq[:], gsq[:], ACT.Exp, scale=-0.5), "gdn_rn")
                on(act, layer, "Gb_mm")
                for p in range(2):
                    say(act.activation(Gb[:, p, :], ps[:, 6 + p, 0:TOK], ACT.Copy), "Gb")
                st.settle()
                say(act.activation(eG[:], Gb[:], ACT.Exp), "eG")
                on(act, layer, "Gdiff")
                say(act.activation(E[:], E[:], ACT.Exp), "E")
                on(act, layer, "Glast")
                say(act.activation(Gd[:], Gd[:], ACT.Exp), "eGd")
                on(act, layer, "gdn_rows_mm", 1)
                st(act.activation(bvt[:].rearrange("q c p t -> q (c p) t"), banks(2, (0, 10)), ACT.Copy))
                on(act, layer, "gdn_rows_mm", 2)
                say(act.activation(gkdt[:].rearrange("q c p t -> q (c p) t"), banks(4, (0, 10)), ACT.Copy), "gdn_rows")
                on(act, layer, "gla_z")
                say(act.activation(ltm, ps[:, 7, 0:TOK], ACT.Abs, bias=P("gb")), "gla_ab")
                st.settle()
                st(act.activation(ltm, ltm, ACT.Exp, scale=-1.0))
                st.settle()
                say(act.activation(ltm, ltm, ACT.Ln, bias=C("one")), "gla_ln")
                for l in range(1, 7):
                    n = TOK if l <= 3 else SEQ
                    on(act, layer, "lD", l)
                    st(act.activation(lE[:, 0:n], lE[:, 0:n], ACT.Abs))
                    st.settle()
                    say(act.activation(lE[:, 0:n], lE[:, 0:n], ACT.Exp, scale=-1.0 / GLA_TAU), "lE")
                on(act, layer, "lBl")
                st(act.activation(lkd, lkd, ACT.Exp, scale=1.0 / GLA_TAU))
                say(act.activation(lB, lB, ACT.Exp, scale=1.0 / GLA_TAU), "leB")
                on(act, layer, "gla_rows_mm", 1)
                st(act.activation(lkt[:].rearrange("q c p t -> q p c t"),
                                  ps[:, 6:8, 0:NC * DK].rearrange("q p (c t) -> q p c t", c=NC), ACT.Copy))
                on(act, layer, "gla_rows_mm", 2)
                say(act.activation(lVt[:].rearrange("q c p t -> q (c p) t"), banks(2, (0, 10)), ACT.Copy), "gla_rows")
                st(act.activation(tiny[:, 11:13], P("lam", 0, 2), ACT.Abs))
                st.settle()
                st(act.activation(tiny[:, 11:13], tiny[:, 11:13], ACT.Exp, scale=-1.0))
                st.settle()
                say(act.activation(tiny[:, 11:13], tiny[:, 11:13], ACT.Ln, bias=C("one")), "sp_lam")
                on(act, layer, "rg_mm")
                for p in range(2):
                    say(act.activation(rr[:, p, :], ps[:, 4 + p, 0:TOK], ACT.Sigmoid, bias=P("ba", p)), "rg_gates")
                for p in range(2):
                    say(act.activation(ri[:, p, :], ps[:, 6 + p, 0:TOK], ACT.Sigmoid, bias=P("bx", p)), "rg_gates")
                on(act, layer, "rg_y")
                st(act.activation(rgt[:], rr[:], ACT.Tanh))
                say(act.activation(rga[:], rr[:], ACT.Exp, scale=-1.0), "rg_a")
                on(act, layer, "rg_b2")
                say(act.activation(rgb[:], rgt[:], ACT.Sqrt), "rg_b")
                on(act, layer, "o_ready", 1)
                say(act.activation(xh[:, 2:4, :], rr[:], ACT.Copy), "o_hi")
                for l in range(1, 6):
                    n = blocks(l)
                    for g in range(2):
                        on(act, layer, "T_mm", 2 * (l - 1) + g + 1)
                        say(act.activation(Tm[:, 10 * g:10 * g + n, :], banks(2 * g, (0, n)), ACT.Copy), "T")
                for g in range(2):
                    on(act, layer, "R0_mm", g + 1)
                    say(act.activation(R0T[g], ps[:, 4 + g, 0:128].rearrange("q (p t) -> q p t", p=2), ACT.Copy), "R0T")
                for c in range(NC):
                    on(act, layer, "rR_mm", c + 1)
                    say(act.activation(RR[0][:, c], ps[:, 0, 0:128].rearrange("q (p t) -> q p t", p=2), ACT.Copy), "rR")
                    on(act, layer, "rU_mm", c + 1)
                    say(act.activation(UU[0][:, c], ps[:, 2, 0:128].rearrange("q (p t) -> q p t", p=2), ACT.Copy, scale=-1.0), "rU")
                for g in range(3):
                    on(act, layer, "out_mm", g + 1)
                    if g:
                        on(act, layer, "yo_done", g)
                    say(act.activation(yo[:], ps[:, 2 * g:2 * g + 2, 0:TOK], ACT.Copy), "yo")
                    on(act, layer, "yo_dec", g + 1)
                    if g == 0:
                        on(act, layer, "mean_read")
                        say(act.activation(ysq[:], yc[:], ACT.Square), "ysq")
                    else:
                        say(act.activation(ysq[:], yo[:], ACT.Square), "ysq")
                    on(act, layer, "var_mm", g + 1)
                    st(act.activation(ysq[:], ps[:, 6:8, 0:TOK], ACT.Ln, bias=C("gne" if g == 0 else "e6"),
                                      scale=1.0 / HD))
                    st.settle()
                    say(act.activation(ysq[:], ysq[:], ACT.Exp, scale=-0.5), "yrs")
                    on(act, layer, "o_ready", g + 2)
                    k0 = (0, 4, 6)[g]
                    say(act.activation(xh[:, k0:k0 + 2, :], yc[:], ACT.Copy), "o_hi")
                for m in range(26, 26 + KT):
                    split_hi(layer, IN0 + RING + m)
                for name in ("shift_kept", "gc_kept", "rgc_kept", "rg_kept"):
                    on(act, layer, name)
                act.dma_start(sout[bass.ds(layer, 1), :, :].rearrange("a q n -> (a q) n"), so[:]).then_inc(state_out.sem, 16)
                on(act, layer, "dec_add")
                for name in ("rM", "gM", "lS"):
                    on(act, layer, name)
                act.dma_start(mout[bass.ds(layer, 1), :, :].rearrange("a q n -> (a q) n"), ms[:]).then_inc(state_out.sem, 16)
                norm_split(layer, 2, "n2")
                rms(layer, 2)
                ffn(layer, 1)
                on(act, layer, x_new)
                on(act, layer, xl_ready)
                act.wait_ge(state_out.sem, layer * 32 + 32)
            for k in range(KT):
                act.activation(nsq[:, k, :], x[:, k, :], ACT.Square).then_inc(sq_ready.sem, 1)
            act.wait_ge(sum_mm.sem, DEPTH * 3 + 1)
            act.activation(lnt[:], ps[:, 7, 0:TOK], ACT.Ln, bias=C("e6"), scale=1.0 / D).then_inc(a_step.sem, 1)
            act.wait_ge(a_step.sem, DEPTH * A_STEPS + 1)
            act.activation(rstd[:], lnt[:], ACT.Exp, scale=-0.5).then_inc(rstd_ready.sem, 1)
            act.wait_ge(state_out.sem, DEPTH * 32)

        @block.vector
        def _(ve):
            tt, ts, stt = ve.tensor_tensor, ve.tensor_scalar, ve.scalar_tensor_tensor

            def split_lo(layer, n, i=0):
                ve.wait_ge(hi_ready.sem, layer * UNITS + i * RING + n + 1)
                s = n % RING
                tt(wl[:, s, :], raw[:, s, :], wh[:, s, :].bitcast(F32), ALU.subtract).then_inc(lo_ready.sem, 1)

            def norm_low(layer, which, name, scale=None):
                for k in range(KT + 2):
                    if which and k < KT:
                        stt(x[:, k, :], ps[:, k, 0:TOK], scale, x[:, k, :], ALU.mult, ALU.add).then_inc(x_new.sem, 1)
                    if k >= 2:
                        j = k - 2
                        ve.wait_ge(xh_ready.sem, layer * 24 + which * KT + j + 1)
                        stt(xl[:, j, :], x[:, j, :], P(name, j), xh[:, j, :].bitcast(F32), ALU.mult, ALU.subtract).then_inc(xl_ready.sem, 1)

            def ffn(layer, f):
                base = f * FFN2
                apart(ve, rstd_ready, rstd_ready.upto(layer, 2 * f + 1))

                def gate(m, i):
                    t = layer * 2 * FT + f * FT + i * 2 + m
                    ve.wait_ge(unit_used.sem, layer * UNITS + i * RING + base + 2 * m + 2)
                    tt(gus[:, m, :], ps[:, 2 * m, 0:TOK], rstd[:], ALU.mult).then_inc(gs_ready.sem, 1)
                    tt(gus[:, 2 + m, :], ps[:, 2 * m + 1, 0:TOK], rstd[:], ALU.mult).then_inc(gu_read.sem, 1)
                    split_lo(layer, base + RING + 2 * m, i)
                    ve.wait_ge(sil_ready.sem, t + 1)
                    ve.wait_ge(gu_read.sem, t + 1)
                    tt(gus[:, m, :], gus[:, m, :], gus[:, 2 + m, :], ALU.mult).then_inc(act_ready.sem, 1)
                    split_lo(layer, base + RING + 2 * m + 1, i)
                    ve.wait_ge(hh_ready.sem, t + 1)
                    at = bass.ds(i * 2 + m, 1)
                    tt(hid_l[:, at, :].rearrange("q a t -> q (a t)"), gus[:, m, :],
                       hid_h[:, at, :].rearrange("q a t -> q (a t)").bitcast(F32), ALU.subtract).then_inc(hl_ready.sem, 1)

                with ve.Fori(0, FT // 2) as i:
                    for m in range(2):
                        gate(m, i)
                splits(layer, base + 2 * FT + RING, min(FT, UNITS - RING - base - 2 * FT), split_lo, ve)
                ve.wait_ge(unit_used.sem, layer * UNITS + base + FFN_UNITS)

            with ve.Fori(0, DEPTH) as layer:
                st = Steps(ve, v_step, layer, plain)

                def say(ins, name):
                    return st(ins, S[name])

                def evac(m):
                    ve.wait_ge(unit_used.sem, layer * UNITS + IN0 + m + 1)
                    src = ps[:, m % 2, 0:TOK]
                    padded = {T_RW: (rwp, 1), T_GDN: (gcp, 3), T_RG: (rgp, 3)}
                    for t0, n in ((T_RW, 7), (T_GDN, 6), (T_RG, 2)):
                        if t0 <= m < t0 + n:
                            buf, pad = padded[t0]
                            st(tt(buf[:, m - t0, pad:pad + SEQ], src[:, 0:SEQ], rstd[:, 0:SEQ], ALU.mult))
                            st(tt(seqs(buf[:, m - t0, :], pad, pad), src[:, SEQ:].rearrange("q (s t) -> q s t", s=DECB),
                                  rstd[:, SEQ:].rearrange("q (s t) -> q s t", s=DECB), ALU.mult), in_read)
                            break
                    else:
                        dst = small if m == T_SMALL else gz[:, m - T_Z, :] if T_Z <= m < T_GLA else \
                            gla[:, m - T_GLA, :] if m < T_GT else gt[:, m - T_GT, :] if m < T_RG else rgg[:, m - T_RGG, :]
                        st(tt(dst, src, rstd[:], ALU.mult), in_read)
                    split_lo(layer, IN0 + RING + m)

                def rw_mix():
                    on(ve, layer, "pads")
                    st.settle()
                    st(tt(xm[:, :, 0:SEQ], rwp[:, :, 0:SEQ], rwp[:, :, 1:1 + SEQ], ALU.subtract))
                    st(tt(seqs(xm, 0), seqs(rwp, 1, 0), seqs(rwp, 1, 1), ALU.subtract))
                    st.settle()
                    for k in range(7):
                        st(stt(xm[:, k, 0:SEQ], xm[:, k, 0:SEQ], P("mu", k), rwp[:, k, 1:1 + SEQ], ALU.mult, ALU.add))
                        say(stt(seqs(xm[:, k, :], 0), seqs(xm[:, k, :], 0), P("mu", k), seqs(rwp[:, k, :], 1, 1), ALU.mult, ALU.add), "xm")
                    st.settle()

                def rw_keys():
                    on(ve, layer, "shift_kept")
                    for p in range(2):
                        say(ts(kk[:, p, :], xm[:, 2 + p, :], P("kk", p), None, ALU.mult), "kkraw")
                    st(ts(tiny[:, 13:15], P("ka", 0, 2), -1.0, 1.0, ALU.mult, ALU.add))
                    on(ve, layer, "ra")
                    st.settle()
                    for p in range(2):
                        st(ts(kmod[:, p, :], ra[:, p, :], P("ka", p), tiny[:, 13 + p:14 + p], ALU.mult, ALU.add))
                    st.settle()
                    st(tt(kmod[:], kmod[:], xm[:, 2:4, :], ALU.mult))
                    st.settle()
                    for p in range(2):
                        say(stt(rtm[:, p, :], xm[:, p, :], P("rk", p), kmod[:, p, :], ALU.mult, ALU.mult), "rkr")

                def rw_decay():
                    on(ve, layer, "sg")
                    for p in range(2):
                        say(ve.tensor_tensor_scan(cum[:, p, :], C("cmask"), sg[:, p, :], 0.0, ALU.mult, ALU.add), "cum")
                    on(ve, layer, "cum")
                    say(tt(sg[:], cum[:], sg[:], ALU.subtract), "prev")

                def rw_scaled():
                    on(ve, layer, "kk_rn")
                    st(tt(kk[:], kk[:], rsq[:], ALU.mult))
                    st.settle()
                    say(tt(ra[:], kk[:], ra[:], ALU.mult), "rb")
                    on(ve, layer, "rw_P")
                    st(tt(kkr[:, :, :, 0, :], chunked(kk), chunked(Pprev), ALU.mult))
                    say(tt(kkr[:, :, :, 1, :], chunked(xm[:, 0:2, :]), chunked(rP), ALU.mult), "rw_ops")
                    say(tt(kPi[:], kmod[:], Pinv[:], ALU.mult), "kPi")
                    on(ve, layer, "rk_sum")
                    say(tt(rw_bonus[:], ps[:, 4:6, 0:TOK], xm[:, 4:6, :], ALU.mult), "bonus")

                def rw_masks():
                    for g, (src_banks, dst) in enumerate((((2, 3, 6), BE), ((4, 5, 7), CD))):
                        on(ve, layer, "rw_pairs", g + 1)
                        for j, bank in enumerate(src_banks):
                            n = 4 if j < 2 else 2
                            say(tt(dst[:, 2 * j:2 * j + n // 2].rearrange("q c p k t -> q (c p) (k t)"),
                                   ps[:, bank, 0:n * 128].rearrange("q (u t) -> q u t", u=n),
                                   tri[:, j // 2].rearrange("q k t -> q (k t)").unsqueeze(1).broadcast_to([128, n, 128]),
                                   ALU.mult), "rw_pairs_read")

                def conv(dst, src, tiles, w, name, bias=None, these=None):
                    for k in range(CONV):
                        if k:
                            st.settle()
                        for j in these or range(tiles):
                            wk = P(w, tiles * k + j)
                            for d_, s_, last_ in ((dst[:, j, 0:SEQ], src[:, j, k:k + SEQ], False),
                                                  (seqs(dst[:, j, :], 0), seqs(src[:, j, :], 3, k), True)):
                                if k == 0 and bias:
                                    ins = ts(d_, s_, wk, P(bias, j), ALU.mult, ALU.add)
                                elif k == 0:
                                    ins = ts(d_, s_, wk, None, ALU.mult)
                                else:
                                    ins = stt(d_, s_, wk, d_, ALU.mult, ALU.add)
                                say(ins, name) if last_ and k == CONV - 1 else st(ins)

                def gdn_conv(*these):
                    on(ve, layer, "kk_sum")
                    on(ve, layer, "rk_sum")
                    on(ve, layer, "bPi")
                    st.settle()
                    conv(cq, gcp, 6, "gcw", "conv", these=these)

                def gdn_gate():
                    R = slice(32, 32 + NH)
                    on(ve, layer, "sp_dt")
                    st(ts(small[R, :], small[R, :], P("dtb")[R], 0.0, ALU.add, ALU.max))
                    st.settle()
                    st(tt(small[R, :], small[R, :], lnt[R, :], ALU.add))
                    st.settle()
                    st(ts(lnt[R, :], small[R, :], tiny[R, 10:11], -1.0, ALU.mult, ALU.mult))
                    st.settle()
                    say(ve.tensor_tensor_scan(small[R, :], C("cmask")[R, :], lnt[R, :], 0.0, ALU.mult, ALU.add), "gcum")

                def last_minus(dst, v, two):
                    pv = v[:, :, 0:SEQ].rearrange("q p (c t) -> q p c t", c=DEC) if two else v[:, 0:SEQ].rearrange("q (c t) -> q c t", c=DEC)
                    dv = seqs(v, 0)
                    pd = dst[:, :, 0:SEQ].rearrange("q p (c t) -> q p c t", c=DEC) if two else dst[:, 0:SEQ].rearrange("q (c t) -> q c t", c=DEC)
                    dd = seqs(dst, 0)
                    yield tt(pd, pv[..., CH - 1:CH].broadcast_to(list(pv.shape)), pv, ALU.subtract)
                    yield tt(dd, dv[..., DECT - 1:DECT].broadcast_to(list(dv.shape)), dv, ALU.subtract)

                def gdn_vectors():
                    on(ve, layer, "gdn_rn")
                    on(ve, layer, "cq")
                    say(stt(cq[:, 0:2, :], cq[:, 0:2, :], HD ** -0.5, gsq[:, 0:2, :], ALU.mult, ALU.mult), "gq")
                    st(tt(cq[:, 2:4, :], cq[:, 2:4, :], gsq[:, 2:4, :], ALU.mult))
                    on(ve, layer, "bb_mm")
                    st.settle()
                    on(ve, layer, "gc_kept")
                    on(ve, layer, "rw_rows_mm", 3)
                    say(tt(kq[:, :, :, 0, :], chunked(cq[:, 2:4, :]), ps[:, 2:4, 0:TOK].rearrange("q p (c t) -> q c p t", c=NC), ALU.mult), "kq")
                    say(tt(vb[:], cq[:, 4:6, :], ps[:, 2:4, 0:TOK], ALU.mult), "vb")
                    on(ve, layer, "Gc_mm")
                    say(ve.tensor_copy(Gc, ps[:, 4, 0:10].rearrange("q (c p) -> q c p", c=NC)), "Gc")
                    on(ve, layer, "Gb")
                    on(ve, layer, "Gc")
                    st(tt(E[:], chunked(Gb), Gc.unsqueeze(3).broadcast_to([128, NC, 2, CH]), ALU.subtract))
                    st.settle()
                    say(ts(E[:], E[:], 0.0, None, ALU.min), "Gdiff")
                    gl = list(last_minus(Gd, Gb, True))
                    st(gl[0]); say(gl[1], "Glast")
                    on(ve, layer, "eG")
                    on(ve, layer, "kq")
                    st(tt(chunked(kbe), kq[:, :, :, 0, :], chunked(eG), ALU.mult))
                    st(tt(qe[:], cq[:, 0:2, :], eG[:], ALU.mult))
                    on(ve, layer, "eGd")
                    say(tt(kd[:], cq[:, 2:4, :], Gd[:], ALU.mult), "kd")
                    on(ve, layer, "KQ_mm")
                    on(ve, layer, "EM")
                    for j, bank in enumerate((5, 6, 7)):
                        n = 4 if j < 2 else 2
                        say(tt(KQ[:, 2 * j:2 * j + n // 2].rearrange("q c p k t -> q (c p) (k t)"),
                               ps[:, bank, 0:n * 128].rearrange("q (u t) -> q u t", u=n),
                               EM[:, 2 * j:2 * j + n // 2].rearrange("q c p k t -> q (c p) (k t)"), ALU.mult), "KQ")

                def gla_all():
                    on(ve, layer, "KQ")
                    on(ve, layer, "gdn_rows")
                    on(ve, layer, "gla_ab")
                    say(ts(gla[:, 0, :], gla[:, 0, :], DK ** -0.5, None, ALU.mult), "gla_q")
                    say(ts(lE, ps[:, 7, 0:TOK], P("gb"), 0.0, ALU.add, ALU.min), "gla_min")
                    on(ve, layer, "gla_ln")
                    st.settle()
                    st(tt(lE, lE, ltm, ALU.subtract))
                    st.settle()
                    st(ve.tensor_tensor_scan(lB, C("cmask"), lE, 0.0, ALU.mult, ALU.add))
                    st.settle()
                    def take(l):
                        nch = NC if l <= 3 else DEC
                        if l:
                            st.settle()
                        apart(ve, S["gla_lev"], S["gla_lev"].upto(layer, l + 1))
                        for p in range(2):
                            say(ve.copy_predicated(At[:, p, 0:nch, :], lev[:, l, :].bitcast(U32).unsqueeze(1).broadcast_to([128, nch, CH]),
                                                   ps[:, 2 + 2 * (l % 2) + p, 0:nch * CH].rearrange("q (c t) -> q c t", c=nch)), "gla_take")
                    on(ve, layer, "At_zero")
                    for l in range(1, 7):
                        s, n = 1 << (l - 1), (TOK if l <= 3 else SEQ)
                        v = lB[:, 0:n].rearrange("q (g t) -> q g t", t=2 * s)
                        if l >= 2:
                            on(ve, layer, "lks", l - 1)
                            on(ve, layer, "lqs", l - 1)
                        say(tt(lE[:, 0:n].rearrange("q (g t) -> q g t", t=2 * s), v, v[:, :, s - 1:s].broadcast_to(list(v.shape)), ALU.subtract), "lD")
                        on(ve, layer, "lE", l)
                        if l >= 3:
                            on(ve, layer, "gla_lev", l - 1)
                        say(tt(lqs[l % 2][:, 0:n], gla[:, 0, 0:n], lE[:, 0:n], ALU.mult), "lqs")
                        take(l - 1)
                    take(6)
                    gl = list(last_minus(lkd, lB, False))
                    st(gl[0]); say(gl[1], "lBl")
                    on(ve, layer, "leB")
                    st(tt(lqe, gla[:, 0, :], lB, ALU.mult))
                    say(tt(lkd, gla[:, 1, :], lkd, ALU.mult), "lkd")

                def gla_chain():
                    on(ve, layer, "lS_mm")
                    on(ve, layer, "chain_zero")
                    ve.wait_ge(state_in.sem, layer * 32 + 32)
                    for c in range(DEC):
                        dst = chain_l[:, c + 1, :] if c + 1 < DEC else Mgla[:, 0, :]
                        say(stt(dst, chain_l[:, c, :], lB[:, c * CH + CH - 1:c * CH + CH], ps[:, 6, c * 64:c * 64 + 64],
                                ALU.mult, ALU.add), "lS")
                        st.settle()


                def rg_conv():
                    on(ve, layer, "gla_rows_mm")
                    st.settle()
                    conv(xc, rgp, 2, "rgcw", "xc", "rgcb")

                def rg_scan():
                    st(ts(tiny[:, 13:15], P("lam", 0, 2), -1.0, 0.0, ALU.mult, ALU.max))
                    on(ve, layer, "sp_lam")
                    st.settle()
                    st(tt(tiny[:, 13:15], tiny[:, 13:15], tiny[:, 11:13], ALU.add))
                    st.settle()
                    on(ve, layer, "rg_gates")
                    for p in range(2):
                        say(ts(rr[:, p, :], rr[:, p, :], tiny[:, 13 + p:14 + p], 8.0, ALU.mult, ALU.mult), "rg_y")
                    on(ve, layer, "rg_a")
                    st(tt(rgb[:], rga[:], rga[:], ALU.mult))
                    st.settle()
                    st(ts(rgb[:], rgb[:], 1.0, None, ALU.add))
                    st.settle()
                    say(stt(rgt[:], rgt[:], 1e-34, rgb[:], ALU.max, ALU.mult), "rg_b2")
                    st(tt(ri[:], ri[:], xc[:], ALU.mult))
                    on(ve, layer, "rg_b")
                    st.settle()
                    st(tt(rgb[:], rgb[:], ri[:], ALU.mult))
                    ve.wait_ge(state_in.sem, layer * 32 + 32)
                    h0 = io(si, SIN, "h", "q (p s) -> q p s", p=2)
                    st(tt(rgt[:, :, 0:DECB], seqs(rga, 0, 0, 1).rearrange("q p s t -> q p (s t)"), h0, ALU.mult))
                    st.settle()
                    first = seqs(rgb, 0, 0, 1).rearrange("q p s t -> q p (s t)")
                    st(tt(first, first, rgt[:, :, 0:DECB], ALU.add))
                    st(ve.memset(rga[:, :, 0:1], 0.0))
                    st(ve.memset(seqs(rga, 0, 0, 1), 0.0))
                    st.settle()
                    for p in range(2):
                        say(ve.tensor_tensor_scan(ri[:, p, :], rga[:, p, :], rgb[:, p, :], 0.0, ALU.mult, ALU.add), "rg_h")
                    st.settle()
                    on(ve, layer, "gates")
                    say(tt(rr[:], ri[:], rgg[:], ALU.mult), "o_ready")

                def o_low(k, src, g):
                    on(ve, layer, "o_hi", g)
                    say(tt(xl[:, k:k + 2, :], src, xh[:, k:k + 2, :].bitcast(F32), ALU.subtract), "o_lo")

                def inverse():
                    eye = lev[:, 0, :].unsqueeze(1).broadcast_to([128, 10, CH])
                    on(ve, layer, "rg_kept")
                    on(ve, layer, "lks")
                    st.settle()

                    def turn(g, n):
                        st.settle()
                        say(ve.transpose(X[:, 10 * g:10 * g + n, :].rearrange("q m s -> q (m s)"),
                                         Y[:, 10 * g:10 * g + n, :].rearrange("q m s -> q (m s)")), "X")

                    for g in range(2):
                        on(ve, layer, "LB", g + 1)
                        say(tt(Y[:, 10 * g:10 * g + 10, :], eye, LB[0][:, 10 * g:10 * g + 10, :], ALU.subtract), "Y")
                        turn(g, 10)
                    for l in range(1, 6):
                        n = blocks(l)
                        for g in range(2):
                            on(ve, layer, "YNY_mm", 2 * (l - 1) + g + 1)
                            y_ = Y[:, 10 * g:10 * g + n, :]
                            say(tt(y_, y_, banks(4 + 2 * g, (0, n)), ALU.subtract), "Y")
                            if l < 5:
                                turn(g, n)

                def recurrences():
                    for c in range(NC):
                        on(ve, layer, "gR_mm", c + 1)
                        if c == 0:
                            on(ve, layer, "T")
                        say(tt(RR[1][:, c], bvt[:, c], ps[:, 1, 0:128].rearrange("q (p t) -> q p t", p=2), ALU.subtract), "gR")
                        on(ve, layer, "gU_mm", c + 1)
                        say(ve.tensor_copy(UU[1][:, c], ps[:, 3, 0:128].rearrange("q (p t) -> q p t", p=2)), "gU")
                        if c == DEC:
                            break
                        t = c * CH + CH - 1
                        for g, (M, D_) in enumerate(((Mrw, rP), (Mgdn, eG))):
                            on(ve, layer, ("rM_mm", "gM_mm")[g], c + 1)
                            for p in range(2):
                                dst = chain_of[g][:, c + 1, p, :] if c + 1 < DEC else M[:, p, 0, :]
                                say(stt(dst, chain_of[g][:, c, p, :], D_[:, p, t:t + 1], ps[:, 6 + g, p * 64:p * 64 + 64], ALU.mult, ALU.add),
                                    ("rM", "gM")[g])
                        st.settle()

                def add_dec(g):
                    on(ve, layer, "yo", g + 1)
                    d_ = yo[:, :, SEQ:]
                    say(tt(d_, d_, ps[:, 2 * g:2 * g + 2, TOK:TOK + CH], ALU.add), "yo_dec")

                def finish(g):
                    add_dec(g)
                    if g == 0:
                        on(ve, layer, "mean_mm")
                        st.settle()
                        say(stt(yc[:], ps[:, 4:6, 0:TOK], -1.0 / HD, yo[:], ALU.mult, ALU.add), "mean_read")
                        on(ve, layer, "yrs", 1)
                        st.settle()
                        say(tt(yc[:], yc[:], ysq[:], ALU.mult), "yo_done")
                        st.settle()
                        for p in range(2):
                            st(ts(yc[:, p, :], yc[:, p, :], P("lnw", p), P("lnb", p), ALU.mult, ALU.add))
                        st.settle()
                        st(tt(yc[:], yc[:], rw_bonus[:], ALU.add))
                        st.settle()
                        say(tt(yc[:], yc[:], rw_g[:], ALU.mult), "o_ready")
                    else:
                        on(ve, layer, "yrs", g + 1)
                        st.settle()
                        say(tt(yc[:], yo[:], ysq[:], ALU.mult), "yo_done")
                        st.settle()
                        say(stt(yc[:], yc[:], P("gnw" if g == 1 else "glw"), (gz if g == 1 else gt)[:], ALU.mult, ALU.mult), "o_ready")
                    o_low((0, 4, 6)[g], yc[:], g + 2)

                def dec_add(g):
                    on(ve, layer, "dec_mm", g + 1)
                    on(ve, layer, "dec_decay", g + 1)
                    b0 = 2 * (g % 2)
                    if g < 2:
                        M = (Mrw, Mgdn)[g]
                        v = M[:, :, 1:, :].rearrange("q p s v -> q p (s v)")
                        say(tt(v, v, ps[:, b0:b0 + 2, :], ALU.add), "dec_add")
                    else:
                        v = Mgla[:, 1:, :].rearrange("q s v -> q (s v)")
                        say(tt(v, v, ps[:, b0, :], ALU.add), "dec_add")

                for n in range(RING):
                    split_lo(layer, n)
                ve.wait_ge(const_in.sem, 32)
                norm_low(layer, 0, "n1")
                ffn(layer, 0)
                norm_low(layer, 1, "nm", 0.5)
                on(ve, layer, rstd_ready, 2)
                ve.wait_ge(unit_used.sem, layer * UNITS + IN0)
                work = {8: [rw_mix], 12: [rw_decay], 13: [rw_keys], 16: [rw_scaled], 20: [rw_masks],
                        21: [lambda: gdn_conv(0, 1)], 22: [lambda: gdn_conv(2)], 23: [lambda: gdn_conv(3)],
                        24: [lambda: gdn_conv(4)], 25: [lambda: gdn_conv(5)]}
                for m in range(IN_TILES):
                    evac(m)
                    for stage in work.get(m, []):
                        stage()
                gdn_gate()
                gdn_vectors()
                gla_all()
                rg_conv()
                rg_scan()
                gla_chain()
                o_low(2, rr[:], 1)
                inverse()
                recurrences()
                finish(0)
                finish(1)
                dec_add(0)
                dec_add(1)
                finish(2)
                dec_add(2)
                for m in range(IN_TILES, IN_TILES + KT):
                    split_lo(layer, IN0 + RING + m)
                ve.wait_ge(unit_used.sem, layer * UNITS + FFN2)
                norm_low(layer, 2, "n2", 1.0)
                ffn(layer, 1)
                for k in range(KT):
                    stt(x[:, k, :], ps[:, k, 0:TOK], 0.5, x[:, k, :], ALU.mult, ALU.add).then_inc(x_new.sem, 1)
            ve.wait_ge(rstd_ready.sem, DEPTH * 3 + 1)
            for k in range(KT):
                stt(x[:, k, :], x[:, k, :], C("nf", k, 1), rstd[:], ALU.mult, ALU.mult).then_inc(x_new.sem, 1)

        @block.gpsimd
        def _(gp):
            with gp.Fori(0, DEPTH) as layer:
                st = Steps(gp, g_step, layer, apart)


                def say(ins, name):
                    return st(ins, S[name])

                def kept(buf, pad, name, dims):
                    n = pad
                    out = so[:, SOUT[name][0]:SOUT[name][0] + SOUT[name][1]].rearrange("q (k s t) -> q k s t", k=dims, s=NSEQ)
                    st(gp.tensor_copy(out[:, :, 0, :], buf[:, :, SEQ:SEQ + pad]))
                    return gp.tensor_copy(out[:, :, 1:, :], seqs(buf, pad, DECT, pad))

                on(gp, layer, rstd_ready, 2)
                apart(gp, state_in, layer * 32 + 32)
                for buf, pad, name, dims in ((rwp, 1, "shift", 7), (gcp, 3, "gc", 6), (rgp, 3, "rgc", 2)):
                    st(gp.memset(buf[:, :, 0:pad], 0.0))
                    src = si[:, SIN[name][0]:SIN[name][0] + SIN[name][1]].rearrange("q (k s t) -> q k s t", k=dims, s=DECB)
                    ins = gp.tensor_copy(seqs(buf, pad, 0, pad), src)
                    say(ins, "pads") if dims == 2 else st(ins)
                say(gp.memset(chain[:], 0.0), "chain_zero")
                on(gp, layer, in_read, 7)
                say(kept(rwp, 1, "shift", 7), "shift_kept")
                on(gp, layer, "kkraw")
                on(gp, layer, "xm")
                say(gp.tensor_tensor(rsq[:], kk[:], kk[:], ALU.mult), "kk_sq")
                on(gp, layer, "rb")
                on(gp, layer, "rw_P")
                say(gp.tensor_tensor(bPi[:], ra[:], Pinv[:], ALU.mult), "bPi")
                st.settle()
                on(gp, layer, "kPi")
                for dst, src in ((kL, kPi), (bL, bPi)):
                    for p in range(2):
                        pe_ = rP[:, p, 0:SEQ].rearrange("q (c t) -> q c t", c=DEC)[:, :, CH - 1:CH].broadcast_to([128, DEC, CH])
                        st(gp.tensor_tensor(dst[:, p, 0:SEQ].rearrange("q (c t) -> q c t", c=DEC),
                                            src[:, p, 0:SEQ].rearrange("q (c t) -> q c t", c=DEC), pe_, ALU.mult))
                        de_ = seqs(rP[:, p, :], 0)[:, :, DECT - 1:DECT].broadcast_to([128, DECB, DECT])
                        say(gp.tensor_tensor(seqs(dst[:, p, :], 0), seqs(src[:, p, :], 0), de_, ALU.mult), "kbL")
                on(gp, layer, in_read, T_SMALL)
                say(kept(gcp, 3, "gc", 6), "gc_kept")
                st.settle()
                on(gp, layer, "gq")
                say(gp.tensor_copy(kq[:, :, :, 1, :], chunked(cq[:, 0:2, :])), "kq_q")
                on(gp, layer, "E")
                for k, (lo, n) in enumerate(((0, 8), (8, 2))):
                    for j in range(2):
                        e_ = E[:].rearrange("q c p t -> q (c p) t")[:, lo:lo + n, :]
                        m_ = tri[:, k, j, :].unsqueeze(1).broadcast_to([128, n, CH])
                        say(gp.tensor_tensor(EM[:].rearrange("q c p k t -> q (c p) k t")[:, lo:lo + n, j, :], e_, m_, ALU.mult), "EM")
                on(gp, layer, "gdn_rows")
                on(gp, layer, "KQ")
                say(gp.memset(At[:], 0.0), "At_zero")
                for l in range(1, 7):
                    n = TOK if l <= 3 else SEQ
                    on(gp, layer, "lE", l)
                    if l >= 3:
                        on(gp, layer, "gla_lev", l - 1)
                    say(gp.tensor_tensor(lks[l % 2][:, 0:n], gla[:, 1, 0:n], lE[:, 0:n], ALU.mult), "lks")
                on(gp, layer, in_read)
                say(kept(rgp, 3, "rgc", 2), "rgc_kept")
                on(gp, layer, "rg_h")
                ho = so[:, SOUT["h"][0]:SOUT["h"][0] + 18].rearrange("q (p s) -> q p s", p=2)
                st(gp.tensor_copy(ho[:, :, 0], ri[:, :, SEQ - 1]))
                say(gp.tensor_copy(ho[:, :, 1:], seqs(ri, 0, DECT - 1, 1).rearrange("q p s t -> q p (s t)")), "rg_kept")
                on(gp, layer, "o_lo", 1)
                for l in range(6):
                    if l == 0:
                        on(gp, layer, "lks")
                        on(gp, layer, "gla_rows_mm", 1)
                    nu = blocks(l)
                    m_ = lev[:, l + 1, :].unsqueeze(1).broadcast_to([128, nu, CH])
                    for g, src in enumerate((BE, KQ)):
                        if l == 2:
                            on(gp, layer, "Y", g + 1)
                        elif l > 2:
                            on(gp, layer, "T_mm", 2 * (l - 3) + g + 1)
                        s_ = src[:].rearrange("q c p k t -> q (c p) k t")[:, 0:nu, 0, :]
                        say(gp.tensor_tensor(LB[l % 2][:, 10 * g:10 * g + nu, :], s_, m_, ALU.mult), "LB")
                sm = C("seqm").unsqueeze(2).broadcast_to([128, DECB, 64])
                for g in range(3):
                    if g == 0:
                        on(gp, layer, "T_mm")
                        on(gp, layer, "rU")
                        on(gp, layer, "gU")
                        srcs = ((VM, rVt), (UM, UU[0]))
                    elif g == 1:
                        on(gp, layer, "dec_mm", 1)
                        srcs = ((UM, UU[1]),)
                    else:
                        srcs = ((VM, lVt),)
                    for j, (dst, src) in enumerate(srcs):
                        for p in range(2):
                            ins = gp.tensor_tensor(dst[:, p], src[:, DEC, p, :].unsqueeze(1).broadcast_to([128, DECB, 64]), sm, ALU.mult)
                            say(ins, "VM") if j == len(srcs) - 1 else st(ins)
                    on(gp, layer, "out_mm", g + 1)
                    if g < 2:
                        for p in range(2):
                            v = (Mrw, Mgdn)[g][:, p, 1:, :]
                            d_ = seqs((rP, eG)[g][:, p, :], 0)[:, :, DECT - 1:DECT].broadcast_to([128, DECB, 64])
                            ins = gp.tensor_tensor(v, v, d_, ALU.mult)
                            say(ins, "dec_decay") if p else st(ins)
                    else:
                        v = Mgla[:, 1:, :]
                        d_ = seqs(lB, 0)[:, :, DECT - 1:DECT].broadcast_to([128, DECB, 64])
                        say(gp.tensor_tensor(v, v, d_, ALU.mult), "dec_decay")
                apart(gp, state_out, layer * 32 + 32)

        for s in [v_step, a_step, g_step, in_read] + list(S.values()):
            assert s.given == s.n, (s.name, s.given)


INS = ("xT", "wts", "par", "cst", "sin", "mst")
OUTS = {"yT": [128, KT, TOK], "sout": [DEPTH, 128, SOUTN], "mout": [DEPTH, 128, MSTN]}


def declare(nc):
    shapes = {"xT": [128, KT, TOK], "wts": [DEPTH * UNITS, 128, 1024], "par": [DEPTH, 128, PARN], "cst": [128, CSTN],
              "sin": [DEPTH, 128, SINN], "mst": [DEPTH, 128, MSTN]}
    args = [nc.dram_tensor(n, shapes[n], F32, kind="ExternalInput").ap() for n in INS]
    args += [nc.dram_tensor(n, s, F32, kind="ExternalOutput").ap() for n, s in OUTS.items()]
    program(nc, *args)


def constants(norm_final):
    c = np.zeros((128, CSTN), np.float32)

    def put(name, a):
        at, n = CST[name]
        c[:, at:at + n] = np.asarray(a, np.float32).reshape(-1, n)

    q, j = np.arange(128), np.arange(64)
    same = (q[:, None] // 64 == q[None, :] // 64)
    put("hones", same)
    put("ones", np.ones((128, 128)))
    s, t = (q % 64)[:, None], j[None, :]
    block = s // DECT == t // DECT
    put("tri", np.stack([s < t, s <= t, (s < t) & block, (s <= t) & block], 1).reshape(128, -1))
    lev = [s == t]
    for l in range(6):
        w = 1 << l
        lev.append((s // (2 * w) == t // (2 * w)) & (s % (2 * w) < w) & (t % (2 * w) >= w))
    put("lev", np.stack(lev, 1).reshape(128, -1))
    tok = np.arange(TOK)
    put("cmask", np.tile(np.where(tok < SEQ, tok % CH, (tok - SEQ) % DECT) != 0, (128, 1)))
    put("seqm", (q % 64)[:, None] // DECT == np.arange(DECB)[None])
    for name, v in (("e6", 1e-6), ("e12", 1e-12), ("gne", GNE), ("one", 1.0)):
        put(name, np.full((128, 1), v))
    at, n = CST["nf"]
    c[:, at:at + n] = norm_final.reshape(KT, 128).T
    return c


def tiles(a):
    return np.moveaxis(a.reshape(*a.shape[:-1], -1, 128), -1, -2)


def lay_out(i):
    i = {k: np.asarray(v) for k, v in i.items()}
    L = DEPTH
    x = np.concatenate([i["x_prompt"][0], i["x_sample"].reshape(-1, D)])
    xT = x.T.reshape(KT, 128, TOK).transpose(1, 0, 2)

    def cols(w):
        return w.reshape(KT, 128, -1, 128).transpose(2, 1, 0, 3).reshape(-1, 128, 1024)

    wts = []
    for l in range(L):
        def ffn(n):
            g, u = cols(i[f"ffn{n}_gate"][l]), cols(i[f"ffn{n}_up"][l])
            return [np.stack([g, u], 1).reshape(-1, 128, 1024), i[f"ffn{n}_down"][l].reshape(FT, 128, 1024)]
        w = i["w_in"][l]
        tw = np.zeros((D, IN_TILES * 128), np.float32)
        for m, at in enumerate(TILE_COL):
            if at is not None:
                tw[:, m * 128:m * 128 + 128] = w[:, at:at + 128]
        b0 = GDN0 + 4 * GW
        for at, src, n in ((0, b0, NH), (32, b0 + NH, NH), (64, GLA_GD, 16)):
            tw[:, T_SMALL * 128 + at:T_SMALL * 128 + at + n] = w[:, src:src + n]
        wts += ffn(1) + [cols(tw), cols(i["w_out"][l])] + ffn(2)
    wts = np.concatenate(wts)

    par = np.zeros((L, 128, PARN), np.float32)

    def put(name, a):
        at, n = PAR[name]
        par[:, :, at:at + n] = a.reshape(L, 128, n)

    for name, key in (("n1", "norm_ffn1"), ("nm", "norm_mix"), ("n2", "norm_ffn2"), ("mu", "rwkv_mu"), ("w0", "rwkv_w0"),
                      ("a0", "rwkv_a0"), ("kk", "rwkv_k_k"), ("ka", "rwkv_k_a"), ("lnw", "rwkv_ln_w"), ("lnb", "rwkv_ln_b"),
                      ("rgcb", "rg_conv_b"), ("ba", "rg_ba"), ("bx", "rg_bx"), ("lam", "rg_lambda"), ("gb", "gla_gb")):
        put(name, tiles(i[key]))
    put("rk", tiles(i["rwkv_r_k"].reshape(L, GW)))
    for name, key in (("rgcw", "rg_conv_w"), ("gcw", "gdn_conv_w")):
        put(name, tiles(i[key]).transpose(0, 2, 1, 3))
    for name, key in (("gnw", "gdn_norm_w"), ("glw", "gla_norm_w")):
        put(name, np.concatenate([i[key], i[key]], 1))
    for name, key in (("alog", "gdn_A_log"), ("dtb", "gdn_dt_bias")):
        par[:, 32:32 + NH, PAR[name][0]] = i[key]
    put("lora", np.concatenate([i["rwkv_w2"], i["rwkv_a2"], i["rwkv_g2"]], 1))
    par[:, 64:80, PAR["glag"][0]:PAR["glag"][0] + 128] = i["gla_g2"]
    for h in range(NH):
        at = PAR["glag"][0] + 64 * h
        par[:, h, at:at + 64] = par[:, 32 + h, at:at + 64] = 1
    for name, key in (("wa", "rg_wa"), ("wx", "rg_wx")):
        for h in range(NH):
            b, p = h % 2, h // 2
            at = PAR[name][0] + 64 * p
            par[:, 64 * b:64 * b + 64, at:at + 64] = i[key][:, h]

    def rows(a, k, n):
        return a.reshape(L, DECB, n, k, 128).transpose(0, 4, 3, 1, 2).reshape(L, 128, -1)

    sin = np.concatenate([rows(i["state_rwkv_shift"], 7, 1), rows(i["state_rglru_conv"], 2, 3), rows(i["state_rglru_h"], 2, 1),
                          rows(i["state_gdn_conv"], 6, 3)], 2)
    mst = np.zeros((L, 128, MSTN), np.float32)

    for name, a in (("rw", i["state_rwkv_wkv"].transpose(0, 1, 2, 4, 3)), ("gdn", i["state_gdn_S"]), ("gla", i["state_gla_S"])):
        at, n = MST[name]
        p = n // NSEQ // 64
        full = np.zeros((L, 128, p, NSEQ, 64), np.float32)
        full[:, :, :, 1:] = a.reshape(L, DECB, p, 128, 64).transpose(0, 3, 2, 1, 4)
        mst[:, :, at:at + n] = full.reshape(L, 128, n)
    return dict(xT=xT, wts=wts, par=par, cst=constants(i["norm_final"]), sin=sin, mst=mst)


def take_back(r):
    y = r["yT"].transpose(1, 0, 2).reshape(D, TOK).T
    L = DEPTH
    so, mo = r["sout"], r["mout"]

    def small_of(name, k, n):
        at, w = SOUT[name]
        a = so[:, :, at:at + w].reshape(L, 128, k, NSEQ, n).transpose(0, 3, 4, 2, 1).reshape(L, NSEQ, n, k * 128)
        return a[:, :, 0] if n == 1 else a

    def matrix_of(name, dk):
        at, w = MST[name]
        p = w // NSEQ // 64
        return mo[:, :, at:at + w].reshape(L, 128, p, NSEQ, 64).transpose(0, 3, 2, 1, 4).reshape(L, NSEQ, NH, dk, 64)

    st = [small_of("shift", 7, 1), matrix_of("rw", 64).transpose(0, 1, 2, 4, 3), small_of("rgc", 2, 3), small_of("h", 2, 1),
          small_of("gc", 6, 3), matrix_of("gdn", 64), matrix_of("gla", DK)]
    c = np.ascontiguousarray
    return tuple([c(y[:SEQ].reshape(1, SEQ, D)), c(y[SEQ:].reshape(DECB, DECT, D))]
                 + [c(s[:, :1]) for s in st] + [c(s[:, 1:]) for s in st])


def kernel(**inputs):
    import concourse.bacc as bacc
    from concourse.bass_utils import run_bass_kernel_spmd
    nc = bacc.Bacc("TRN2", target_bir_lowering=False, num_devices=1)
    declare(nc)
    arrays = {k: np.ascontiguousarray(v) for k, v in lay_out(inputs).items()}
    r = run_bass_kernel_spmd(nc, [arrays], core_ids=[0])
    return take_back(r.results[0])
```

```python
from contextlib import ExitStack

import numpy as np

import concourse.bass as bass
from concourse import mybir

F32, F32R, U32 = mybir.dt.float32, mybir.dt.float32r, mybir.dt.uint32
ACT = mybir.ActivationFunctionType
ALU = mybir.AluOpType

D, DEPTH, SEQ, DECB, DECT = 1024, 2, 256, 8, 8
TOK = SEQ + DECB * DECT
GW, HD, NH, DK = 256, 64, 4, 32
CH = 64
NC = TOK // CH
DEC = NC - 1
FF = 2816
KT, FT = D // 128, FF // 128
NSEQ = 1 + DECB
CONV = 4
GNE = 64e-5
WDEC = float(np.exp(-0.5))
GLA_TAU = 16.0

RING = 4
FFN_UNITS = 3 * FT
IN_TILES = 26
IN0 = FFN_UNITS
OUT0 = IN0 + IN_TILES
FFN2 = OUT0 + KT
UNITS = FFN2 + FFN_UNITS
assert FFN2 % RING == 0 and (2 * FT) % RING == 0

RW_COLS, RG_COLS, GDN_COLS = 3 * GW + 128, 2 * GW, 4 * GW + 2 * NH
RG0, GDN0, GLA0 = RW_COLS, RW_COLS + RG_COLS, RW_COLS + RG_COLS + GDN_COLS
GLA_GD = GLA0 + 2 * NH * DK + 2 * GW
T_RW, T_GDN, T_SMALL, T_Z, T_GLA, T_GT, T_RG, T_RGG = 0, 7, 13, 14, 16, 20, 22, 24
TILE_COL = ([128 * i for i in range(7)] + [GDN0 + 128 * i for i in range(6)] + [None]
            + [GDN0 + 3 * GW + 128 * i for i in range(2)] + [GLA0 + 128 * i for i in range(6)]
            + [RG0 + 128 * i for i in range(4)])


def columns(spec):
    at, out = 0, {}
    for name, n in spec:
        out[name] = (at, n)
        at += n
    return out, at


PAR, PARN = columns([
    ("n1", 8), ("nm", 8), ("n2", 8), ("mu", 7), ("w0", 2), ("a0", 2), ("kk", 2), ("ka", 2), ("rk", 2),
    ("lnw", 2), ("lnb", 2), ("rgcw", 8), ("rgcb", 2), ("ba", 2), ("bx", 2), ("lam", 2), ("gcw", 24),
    ("gnw", 1), ("glw", 1), ("alog", 1), ("dtb", 1), ("gb", 1), ("lora", 256), ("glag", 256),
    ("wa", 128), ("wx", 128)])
CST, CSTN = columns([
    ("hones", 128), ("ones", 128), ("tri", 256),
    ("lev", 7 * 64), ("cmask", TOK), ("seqm", 8), ("e6", 1), ("e12", 1), ("gne", 1),
    ("one", 1), ("nf", 8)])
SIN, SINN = columns([("shift", 7 * 8), ("rgc", 2 * 8 * 3), ("h", 2 * 8), ("gc", 6 * 8 * 3)])
SOUT, SOUTN = columns([("shift", 7 * 9), ("rgc", 2 * 9 * 3), ("h", 2 * 9), ("gc", 6 * 9 * 3)])
MST, MSTN = columns([("rw", 2 * NSEQ * 64), ("gdn", 2 * NSEQ * 64), ("gla", NSEQ * 64)])

RWP = 1 + SEQ + DECB * (1 + DECT)
CVP = 3 + SEQ + DECB * (3 + DECT)


MIX_SIGNALS = {
    "pads": 1, "chain_zero": 1, "xm": 7, "lora_in": 1, "lora_mm": 3, "sg": 2, "ra": 2,
    "rw_gc": 2, "shift_kept": 1, "kkraw": 2, "kk_sq": 1, "rkr": 2, "kk_sum": 1, "rk_sum": 1, "cum": 2, "prev": 1,
    "rw_P": 1, "kk_rn": 1, "rb": 1, "rw_ops": 1, "kPi": 1, "bPi": 1, "bonus": 1, "kbL": 4,
    "rw_pairs": 2, "rw_pairs_read": 6,
    "rw_rows_mm": 3, "rw_rows": 1, "conv": 6, "cq": 1,
    "gates": 1, "beta": 1, "gsq": 1, "sp_dt": 1, "gdn_sum": 1, "gdn_rn": 1, "gcum": 1, "Gb_mm": 1, "Gb": 2,
    "eG": 1, "bb_mm": 1, "Gc_mm": 1, "Gc": 1, "gq": 1, "kq": 1, "kq_q": 1, "vb": 1, "Gdiff": 1, "E": 1, "Glast": 1,
    "eGd": 1, "kd": 1, "EM": 4, "KQ_mm": 1, "KQ": 3, "gdn_rows_mm": 2, "gdn_rows": 1, "gc_kept": 1,
    "gla_z": 1, "gla_ab": 1, "gla_q": 1, "gla_min": 1, "gla_ln": 1, "At_zero": 1, "lD": 6, "lE": 6, "lqs": 6,
    "lks": 6, "gla_lev": 7, "gla_take": 14, "lBl": 1, "leB": 1, "lkd": 1, "gla_rows_mm": 2, "gla_rows": 1,
    "xc": 2, "rg_mm": 2, "rg_gates": 4, "sp_lam": 1, "rg_y": 2, "rg_a": 1, "rg_b2": 1, "rg_b": 1, "rg_h": 2,
    "rg_kept": 1, "rgc_kept": 1, "lS_mm": 1, "lS": 4, "o_ready": 4, "o_hi": 4, "o_lo": 4, "LB0": 6, "LB1": 6, "inv_mm0": 10, "inv_mm1": 10, "XY0": 11, "XY1": 11, "T0": 5, "T1": 5,
    "R0_mm": 2, "R0T": 2, "rR_mm": 5, "gR_mm": 5, "rR": 5,
    "gR": 5, "rU_mm": 5, "gU_mm": 5, "rU": 5, "gU": 5, "rM_mm": 4, "gM_mm": 4, "rM": 8, "gM": 8, "out_mm": 3,
    "yo": 3, "yo_dec": 3, "ysq0": 1, "ysq1": 1, "ysq2": 1, "yrs": 2, "mean_mm": 1, "mean_read": 1, "var_mm": 3, "VM": 6, "dec_mm": 3,
    "dec_decay": 3, "dec_add": 3,
}
V_STEPS, A_STEPS, G_STEPS = 114, 34, 17


class Signal:

    def __init__(self, ctx, nc, name, n=1):
        self.sem, self.n, self.given, self.name = ctx.enter_context(nc.semaphore(name)), n, 0, name

    def upto(self, layer, k=None):
        return layer * self.n + (self.n if k is None else k)


class Steps:

    def __init__(self, eng, own, layer, wait):
        self.eng, self.own, self.layer, self.last, self.wait = eng, own, layer, None, wait

    def __call__(self, ins, sig=None):
        sig = sig or self.own
        ins.then_inc(sig.sem, 1)
        sig.given += 1
        self.last = (sig, sig.given)
        return ins

    def settle(self):
        sig, k = self.last
        self.wait(self.eng, sig, sig.upto(self.layer, k))


def program(nc, xT, wts, par, cst, sin, mst, yT, sout, mout):
    with ExitStack() as ctx:
        def sb(name, shape, dt=F32):
            return ctx.enter_context(nc.sbuf_tensor(name, shape, dt))

        def signal(name, n=1):
            s = Signal(ctx, nc, name, n)
            signals.append(s)
            return s

        signals = []
        x = sb("x", [128, KT, TOK])
        xh = sb("xh", [128, KT, TOK], F32R)
        xl = sb("xl", [128, KT, TOK], F32R)
        raw = sb("raw", [128, RING, 1024])
        wh = sb("wh", [128, RING, 1024], F32R)
        wl = sb("wl", [128, RING, 1024], F32R)
        pr = sb("pr", [128, PARN])
        cs = sb("cs", [128, CSTN])
        si = sb("si", [128, SINN])
        so = sb("so", [128, SOUTN])
        ms = sb("ms", [128, MSTN])
        chain = sb("chain", [128, 2 * 4 * 128 + 4 * 64])
        rstd = sb("rstd", [128, TOK])
        lnt = sb("lnt", [128, TOK])
        tiny = sb("tiny", [128, 16])
        with nc.sbuf_tensor("hid_h", [128, FT, TOK], F32R) as hid_h, \
                nc.sbuf_tensor("hid_l", [128, FT, TOK], F32R) as hid_l, \
                nc.sbuf_tensor("gus", [128, 4, TOK], F32) as gus:
            pass
        ar = sb("ar", [128, 80 * TOK])
        ps = ctx.enter_context(nc.psum_tensor("ps", [128, 8, 512], F32))

        def A(u, n, pat=None, **kw):
            v = ar[:, u * TOK:u * TOK + n]
            return v.rearrange(pat, **kw) if pat else v

        def P(name, i=0, n=1):
            return pr[:, PAR[name][0] + i:PAR[name][0] + i + n]

        def C(name, i=0, n=None):
            at, w = CST[name]
            return cs[:, at + i:at + i + (w if n is None else n)]

        PT = "q (p t) -> q p t"
        CP = "q (c p t) -> q c p t"
        rw_g, rw_bonus, rP = (A(u, 640, PT, p=2) for u in (0, 2, 4))
        kkr = A(6, 1280, "q (c p k t) -> q c p k t", c=NC, p=2, k=2)
        BE = A(10, 1280, "q (c p k t) -> q c p k t", c=NC, p=2, k=2)
        CD = A(14, 1280, "q (c p k t) -> q c p k t", c=NC, p=2, k=2)
        rVt, kLt, bLt = (A(u, 640, CP, c=NC, p=2) for u in (18, 20, 22))
        gz, eG, kbe, qe = (A(u, 640, PT, p=2) for u in (24, 26, 28, 30))
        KQ = A(32, 1280, "q (c p k t) -> q c p k t", c=NC, p=2, k=2)
        bvt, gkdt = (A(u, 640, CP, c=NC, p=2) for u in (36, 38))
        gt = A(40, 640, PT, p=2)
        small = A(42, 320)
        gla = A(43, 1280, "q (k t) -> q k t", k=4)
        rgp = A(47, 2 * CVP, PT, p=2)
        rgg = A(50, 640, PT, p=2)
        rwp = A(52, 7 * RWP, PT, p=7)
        xm = A(60, 7 * TOK, PT, p=7)
        sg, cum, Pinv = (A(u, 640, PT, p=2) for u in (67, 69, 71))
        Pprev, kmod, bPi, kPi, bL, kL, kk = (A(u, 640, PT, p=2) for u in (26, 28, 30, 32, 34, 36, 38))
        ra, rsq, rtm = (A(u, 640, PT, p=2) for u in (52, 54, 56))
        gcp = A(73, 6 * CVP, PT, p=6)
        cq = A(52, 6 * TOK, PT, p=6)
        gsq = A(64, 4 * TOK, PT, p=4)
        Gb, Gd, kd, vb = (A(u, 640, PT, p=2) for u in (62, 78, 74, 76))
        E = A(64, 640, CP, c=NC, p=2)
        EM = A(66, 1280, "q (c p k t) -> q c p k t", c=NC, p=2, k=2)
        kq = A(70, 1280, "q (c p k t) -> q c p k t", c=NC, p=2, k=2)
        Gc = tiny[:, 0:10].rearrange("q (c p) -> q c p", c=NC)
        At = A(72, 640, "q (p c t) -> q p c t", p=2, c=NC)
        lqe = A(74, 320)
        lVt = A(75, 640, CP, c=NC, p=2)
        lkt = A(77, 320, "q (c p t) -> q c p t", c=NC, p=2)
        lB, lE, lkd, ltm = (A(u, 320) for u in (78, 61, 66, 67))
        lqs, lks = [A(62, 320), A(63, 320)], [A(64, 320), A(65, 320)]
        xc, rr, ri, rga, rgb, rgt = (A(u, 640, PT, p=2) for u in (52, 54, 56, 58, 52, 47))
        slots = raw[:].rearrange("q s c -> q (s c)")
        X, Y, Tm = ([slots[:, (2 * i + g) * 640:(2 * i + g + 1) * 640].rearrange("q (m s) -> q m s", m=10) for g in range(2)]
                    for i in range(3))
        LB = [A(u, 640, "q (m s) -> q m s", m=10) for u in (58, 70)]
        RR = [A(u, 640, CP, c=NC, p=2) for u in (60, 64)]
        UU = [A(u, 640, CP, c=NC, p=2) for u in (62, 66)]
        VM = A(52, 1024, "q (p s v) -> q p s v", p=2, s=DECB)
        UM = A(56, 1024, "q (p s v) -> q p s v", p=2, s=DECB)
        yo = [A(u, 640, PT, p=2) for u in (43, 45, 47)]
        ysq = [A(u, 640, PT, p=2) for u in (49, 68, 70)]
        ysq_12 = A(68, 1280, PT, p=4)
        R0T = [A(51, 256, "q (g p t) -> q g p t", g=2, p=2)[:, g] for g in range(2)]
        nsq = A(49, 8 * TOK, PT, p=8)

        def mstate(name, p=2):
            at, n = MST[name]
            return ms[:, at:at + n].rearrange("q (p s v) -> q p s v", p=p, s=NSEQ)

        Mrw, Mgdn = mstate("rw"), mstate("gdn")
        Mgla = mstate("gla", 1)[:, 0]
        chain_of = [chain[:, 512 * i:512 * i + 512].rearrange("q (c p v) -> q c p v", c=4, p=2) for i in range(2)]
        chain_l = chain[:, 1024:1280].rearrange("q (c v) -> q c v", c=4)

        def io(t, spec, name, pat, **kw):
            at, n = spec[name]
            return t[:, at:at + n].rearrange(pat, **kw)

        tri = C("tri").rearrange("q (d k t) -> q d k t", d=2, k=2)
        lev = C("lev").rearrange("q (l t) -> q l t", l=7)
        sel = P("glag", 0, 256).rearrange("q (p m) -> q p m", p=2)
        wrg = [P("wa", 0, 128).rearrange("q (p m) -> q p m", p=2), P("wx", 0, 128).rearrange("q (p m) -> q p m", p=2)]

        half = [slice(0, 64), slice(64, 128)]
        I64 = [lev[half[b], 0, :] for b in range(2)]

        def seqs(v, pad, first=0, n=DECT):
            at = (pad + SEQ) if pad else SEQ
            flat = v[..., at:at + DECB * (DECT + pad)]
            if len(v.shape) == 2:
                return flat.rearrange("q (s t) -> q s t", s=DECB)[:, :, first:first + n]
            return flat.rearrange("q p (s t) -> q p s t", s=DECB)[:, :, :, first:first + n]

        def chunked(v):
            return v.rearrange("q p (c t) -> q c p t", c=NC)

        def splits(layer, first, count, split, eng):
            with eng.Fori(0, count // RING) as i:
                for k in range(RING):
                    split(layer, first + k, i)
            for k in range(count // RING * RING, count):
                split(layer, first + k)

        def banks(bank, runs, w=64):
            lo, hi = runs
            flat = ps[:, bank:bank + 3, :].rearrange("q b t -> q (b t)") if bank <= 5 else \
                ps[:, bank:8, :].rearrange("q b t -> q (b t)")
            return flat[:, lo * w:hi * w].rearrange("q (u t) -> q u t", u=hi - lo)

        DEC_BANK = (6, 4, 3)

        def blocks(level):
            return 10 if level <= 2 else 8

        raw_in = [signal(f"raw_in{s}") for s in range(RING)]
        const_in, y_out = signal("const_in"), signal("y_out")
        par_in, state_in, state_out = (signal(n) for n in ("par_in", "state_in", "state_out"))
        hi_ready, lo_ready = signal("hi_ready", UNITS), signal("lo_ready", UNITS)
        unit_used = signal("unit_used", UNITS)
        v_step, a_step, g_step = signal("v_step", V_STEPS), signal("a_step", A_STEPS), signal("g_step", G_STEPS)
        sq_ready, xh_ready, xl_ready, x_new = (signal(n, 24) for n in ("sq_ready", "xh_ready", "xl_ready", "x_new"))
        sum_mm, rstd_ready = signal("sum_mm", 3), signal("rstd_ready", 3)
        gs_ready, gu_read, sil_ready, act_ready, hh_ready, hl_ready = (
            signal(n, 2 * FT) for n in ("gs_ready", "gu_read", "sil_ready", "act_ready", "hh_ready", "hl_ready"))
        in_read = signal("in_read", IN_TILES)
        S = {name: signal(name, n) for name, n in MIX_SIGNALS.items()}

        passed = signal("passed")
        OWN_WAITS = (mybir.EngineType.PE, mybir.EngineType.Pool)

        def apart(eng, s, value):
            eng.wait_ge(s.sem, value).then_inc(passed.sem, 1)

        def plain(eng, s, value):
            eng.wait_ge(s.sem, value)

        def on(eng, layer, s, k=None):
            s = S[s] if isinstance(s, str) else s
            apart(eng, s, s.upto(layer, k)) if eng.engine in OWN_WAITS else eng.wait_ge(s.sem, s.upto(layer, k))

        def per_slot(s):
            return len(range(s, UNITS, RING))

        def raw_landed(eng, layer, n, i):
            s = n % RING
            eng.wait_ge(raw_in[s].sem, (layer * per_slot(s) + i + n // RING + 1) * 16)

        def slot_free(eng, layer, n, i):
            if n >= RING:
                eng.wait_ge(unit_used.sem, layer * UNITS + i * RING + n - RING + 1)

        block = ctx.enter_context(nc.Block())

        @block.sync
        def _(sp):
            sp.dma_start(cs[:], cst).then_inc(const_in.sem, 16)
            sp.dma_start(x[:], xT).then_inc(const_in.sem, 16)

            def load(layer, n, i=0):
                s = n % RING
                unit = layer * UNITS + i * RING + n
                sp.dma_start(raw[:, s, :], wts[bass.ds(unit, 1), :, :].rearrange("n p c -> (n p) c")) \
                    .then_inc(raw_in[s].sem, 16)

            with sp.Fori(0, DEPTH) as layer:
                for n in range(RING):
                    load(layer, n)
                held = (OUT0 + RING) // RING - 1
                assert (OUT0 + RING) % RING == 0
                for lo, hi in ((0, held), (held, UNITS // RING - 1)):
                    if lo:
                        apart(sp, S["rU_mm"], S["rU_mm"].upto(layer))
                        apart(sp, S["gU_mm"], S["gU_mm"].upto(layer))
                    with sp.Fori(lo, hi) as i:
                        for n in range(RING, 2 * RING):
                            sp.wait_ge(lo_ready.sem, layer * UNITS + i * RING + n - RING + 1)
                            load(layer, n, i)
                for n in range(UNITS // RING * RING, UNITS):
                    sp.wait_ge(lo_ready.sem, layer * UNITS + n - RING + 1)
                    load(layer, n)
                apart(sp, lo_ready, layer * UNITS + UNITS)
            sp.wait_ge(x_new.sem, DEPTH * 24 + KT)
            sp.dma_start(yT, x[:]).then_inc(y_out.sem, 16)
            sp.wait_ge(y_out.sem, 16)

        @block.tensor
        def _(pe):
            def put(ins, name):
                ins.then_inc(S[name].sem, 1)
                S[name].given += 1

            def three(out, a, b, rh, rl, start, stop):
                pe.matmul(out, a, rh, start=start, stop=False)
                pe.matmul(out, a, rl, start=False, stop=False)
                return pe.matmul(out, b, rh, start=False, stop=stop)

            def wsl(s, k):
                return wh[:, s, k * 128:(k + 1) * 128], wl[:, s, k * 128:(k + 1) * 128]

            def tile_mm(layer, n, bank, i=0):
                pe.wait_ge(lo_ready.sem, layer * UNITS + i * RING + n + 1)
                for k in range(KT):
                    ins = three(ps[:, bank, 0:TOK], *wsl(n % RING, k), xh[:, k, :], xl[:, k, :], k == 0, k == KT - 1)
                ins.then_inc(unit_used.sem, 1)

            def norm_sums(layer, which):
                for k in range(KT):
                    pe.wait_ge(sq_ready.sem, layer * 24 + which * KT + k + 1)
                    ins = pe.matmul(ps[:, 7, 0:TOK], C("ones"), nsq[:, k, :], start=(k == 0), stop=(k == KT - 1))
                ins.then_inc(sum_mm.sem, 1)

            def first_tiles(layer, base, which):
                for k in range(KT):
                    if k == KT - 2:
                        norm_sums(layer, which)
                    pe.wait_ge(xl_ready.sem, layer * 24 + which * KT + k + 1)
                    for m in range(RING):
                        if k == 0:
                            pe.wait_ge(lo_ready.sem, layer * UNITS + base + m + 1)
                        s = (base + m) % RING
                        ins = three(ps[:, m, 0:TOK], *wsl(s, k), xh[:, k, :], xl[:, k, :], k == 0, k == KT - 1)
                        if k == KT - 1:
                            ins.then_inc(unit_used.sem, 1)

            def ffn(layer, f):
                base = f * FFN2

                def gate_up(i, m):
                    tile_mm(layer, base + 2 * m, 2 * m, i)
                    tile_mm(layer, base + 2 * m + 1, 2 * m + 1, i)

                first_tiles(layer, base, 2 * f)
                with pe.Fori(1, FT // 2) as i:
                    for m in range(2):
                        pe.wait_ge(gu_read.sem, layer * 2 * FT + f * FT + i * 2 + m - 1)
                        gate_up(i, m)
                on(pe, layer, hl_ready, f * FT + FT - 3)
                on(pe, layer, gu_read, f * FT + FT - 1)

                def down(k, i=0, start=False, stop=False):
                    n = base + 2 * FT + k
                    pe.wait_ge(lo_ready.sem, layer * UNITS + i * RING + n + 1)
                    at = bass.ds(i * RING + k, 1)
                    rh = hid_h[:, at, :].rearrange("q a t -> q (a t)")
                    rl = hid_l[:, at, :].rearrange("q a t -> q (a t)")
                    for m in (0, 1, 4, 5, 6, 7, 2, 3):
                        if start and m == 2:
                            on(pe, layer, gu_read, (f + 1) * FT)
                        ins = three(ps[:, m, 0:TOK], *wsl(n % RING, m), rh, rl, start, stop)
                    ins.then_inc(unit_used.sem, 1)

                down(0, start=True)
                on(pe, layer, hl_ready, (f + 1) * FT)
                with pe.Fori(0, (FT - 2) // RING) as i:
                    for k in range(1, 1 + RING):
                        down(k, i)
                down(FT - 1, stop=True)

            def each(fn, chunks=range(NC)):
                for c in chunks:
                    for p in range(2):
                        for b in range(2):
                            ins = fn(c, p, b)
                return ins

            def cht(v, c, p, b):
                return v[half[b], p, c * CH:(c + 1) * CH]

            def lora(layer):
                on(pe, layer, "lora_in")
                lo = P("lora", 0, 256)
                for rows, bank in ((slice(0, 32), 2), (slice(32, 64), 4), (slice(64, 128), 6)):
                    for p in range(2):
                        ins = pe.matmul(ps[:, bank + p, 0:TOK], lo[rows, p * 128:p * 128 + 128], xm[rows, 6, :], start=True, stop=True)
                    put(ins, "lora_mm")

            def rw_sums(layer):
                on(pe, layer, "sg")
                on(pe, layer, "kk_sq")
                for p in range(2):
                    ins = pe.matmul(ps[:, 2 + p, 0:TOK], C("hones"), rsq[:, p, :], start=True, stop=True)
                put(ins, "kk_sum")
                on(pe, layer, "ra")
                on(pe, layer, "rkr")
                for p in range(2):
                    ins = pe.matmul(ps[:, 4 + p, 0:TOK], C("hones"), rtm[:, p, :], start=True, stop=True)
                put(ins, "rk_sum")

            def products(src, rhs, three_banks, name):
                def f(c, p, b):
                    return pe.matmul(ps[half[b], three_banks[c // 2], ((c % 2) * 2 + p) * 128:][:, 0:128],
                                     cht(src, c, p, b), rhs[half[b], c, p].rearrange("q k t -> q (k t)"),
                                     start=True, stop=True)
                put(each(f), name)

            def rw_products(layer):
                on(pe, layer, "rw_ops")
                on(pe, layer, "bPi")
                on(pe, layer, "kPi")
                on(pe, layer, "rw_gc")
                on(pe, layer, "bonus")
                on(pe, layer, "kk_rn")
                products(bPi, kkr, (2, 3, 6), "rw_pairs")
                products(kPi, kkr, (4, 5, 7), "rw_pairs")

            def to_rows(src, bank, name):
                def f(c, p, b):
                    u = c * 2 + p
                    return pe.matmul(ps[half[b], bank + u // 8, (u % 8) * 64:(u % 8) * 64 + 64], cht(src, c, p, b), I64[b],
                                     start=True, stop=True)
                put(each(f), name)

            def rw_rows(layer):
                on(pe, layer, "rw_pairs_read")
                on(pe, layer, "kbL")
                to_rows(xm[:, 4:6], 2, "rw_rows_mm")
                to_rows(kL, 4, "rw_rows_mm")
                to_rows(bL, 6, "rw_rows_mm")

            def gdn_sums(layer):
                on(pe, layer, "gsq")
                on(pe, layer, "rw_rows")
                for k in range(4):
                    ins = pe.matmul(ps[:, 2 + k, 0:TOK], C("hones"), gsq[:, k, :], start=True, stop=True)
                put(ins, "gdn_sum")

            def gdn_bcast(layer):
                on(pe, layer, "gcum")
                R = slice(32, 32 + NH)
                for p in range(2):
                    ins = pe.matmul(ps[:, 6 + p, 0:TOK], sel[R, p, :], small[R, :], start=True, stop=True)
                put(ins, "Gb_mm")
                on(pe, layer, "gdn_rn")
                on(pe, layer, "beta")
                for p in range(2):
                    ins = pe.matmul(ps[:, 2 + p, 0:TOK], sel[0:NH, p, :], small[0:NH, :], start=True, stop=True)
                put(ins, "bb_mm")
                on(pe, layer, "Gb")
                def f(c, p, b):
                    return pe.matmul(ps[half[b], 4, c * 2 + p:c * 2 + p + 1], cht(Gb, c, p, b), I64[b][:, 0:1], start=True, stop=True)
                put(each(f), "Gc_mm")

            def gdn_products(layer):
                on(pe, layer, "kq")
                on(pe, layer, "kq_q")
                on(pe, layer, "Gb")
                products(cq[:, 2:4], kq, (5, 6, 7), "KQ_mm")

            def gdn_rows(layer):
                on(pe, layer, "vb")
                to_rows(vb, 2, "gdn_rows_mm")
                on(pe, layer, "kd")
                on(pe, layer, "KQ")
                on(pe, layer, "Gc")
                to_rows(kd, 4, "gdn_rows_mm")

            def gla_gate(layer):
                on(pe, layer, "KQ")
                ins = pe.matmul(ps[:, 7, 0:TOK], P("glag", 0, 128)[64:80, :], small[64:80, :], start=True, stop=True)
                put(ins, "gla_z")

            def gla_level(layer, l):
                if l == 0:
                    on(pe, layer, "gdn_rows")
                    on(pe, layer, "gla_q")
                else:
                    on(pe, layer, "lqs", l)
                    on(pe, layer, "lks", l)
                    on(pe, layer, "gla_take", 2 * l)
                kk_, qq_ = (gla[:, 1, :], gla[:, 0, :]) if l == 0 else (lks[l % 2], lqs[l % 2])
                for c in range(NC if l <= 3 else DEC):
                    for h in range(NH):
                        r = slice(DK * h, DK * h + DK)
                        t = slice(c * CH, (c + 1) * CH)
                        ins = pe.matmul(ps[half[h % 2], 4 + h // 2, t], kk_[r, t], qq_[r, t], start=True, stop=True)
                put(ins, "gla_lev")

            def gla_rows(layer):
                on(pe, layer, "lkd")
                on(pe, layer, "gla_take")
                on(pe, layer, "rg_gates")
                for c in range(NC):
                    for h in range(NH):
                        r = slice(DK * h, DK * h + DK)
                        ins = pe.matmul(ps[half[h % 2], 6 + h // 2, c * DK:c * DK + DK],
                                        lkd[r, c * CH:(c + 1) * CH], lev[r, 0, DK * (h % 2):DK * (h % 2) + DK], start=True, stop=True)
                put(ins, "gla_rows_mm")
                to_rows(gla[:, 2:4], 4, "gla_rows_mm")

            def gla_states(layer):
                on(pe, layer, "gla_rows")
                for h in range(NH):
                    b, p, r = h % 2, h // 2, slice(DK * h, DK * h + DK)
                    for c in range(DEC):
                        ins = pe.matmul(ps[r, 6, c * 64:c * 64 + 64], lkt[half[b], c, p, :], lVt[half[b], c, p, :], start=True, stop=True)
                put(ins, "lS_mm")

            def rg_gate(layer, g):
                if g == 0:
                    on(pe, layer, "xc")
                    on(pe, layer, "gla_ab")
                    on(pe, layer, "gla_min")
                else:
                    on(pe, layer, "rg_gates", 2)
                for p in range(2):
                    for b in range(2):
                        ins = pe.matmul(ps[half[b], 6 + p, 0:TOK], wrg[g][half[b], p, :], xc[half[b], p, :], start=True, stop=True)
                put(ins, "rg_mm")

            def inverse_unit(g, m, b):
                return ps[half[b], 2 * g + m // 8, (m % 8) * 64:(m % 8) * 64 + 64]

            def inverse_t(layer, g, l):
                on(pe, layer, f"LB{g}", l + 1)
                on(pe, layer, f"XY{g}", 2 * l)
                if l == 1:
                    on(pe, layer, *((in_read,) if g == 0 else ("gdn_rows",)))
                for m in range(blocks(l)):
                    for b in range(2):
                        ins = pe.matmul(inverse_unit(g, m, b), LB[g][half[b], m], X[g][half[b], m], start=True, stop=True)
                put(ins, f"inv_mm{g}")

            def inverse_y(layer, g, l):
                on(pe, layer, f"T{g}", l)
                for m in range(blocks(l)):
                    for b in range(2):
                        ins = pe.matmul(inverse_unit(g, m, b), Tm[g][half[b], m], Y[g][half[b], m], start=True, stop=True)
                put(ins, f"inv_mm{g}")

            def recurrences(layer):
                on(pe, layer, "XY0")
                on(pe, layer, "XY1")
                apart(pe, state_in, layer * 32 + 32)
                for g, M in enumerate((Mrw, Mgdn)):
                    for p in range(2):
                        for b in range(2):
                            for q in range(DECB):
                                t = slice(q * 8, q * 8 + 8)
                                rhs = kkr[half[b], DEC, p, 0, t] if g == 0 else kbe[half[b], p, SEQ:][:, t]
                                ins = pe.matmul(ps[half[b], 4 + g, p * 64 + q * 8:p * 64 + q * 8 + 8], M[half[b], p, 1 + q, :],
                                                rhs, start=True, stop=True)
                    put(ins, "R0_mm")
                on(pe, layer, "chain_zero")
                for c in range(NC):
                    for g in range(2):
                        if c == DEC:
                            on(pe, layer, "R0T", g + 1)
                        if c:
                            on(pe, layer, ("rM", "gM")[g], 2 * min(c, DEC))
                            on(pe, layer, ("rR", "gR")[g], c)
                        for p in range(2):
                            for b in range(2):
                                o = ps[half[b], g, p * 64:p * 64 + 64]
                                if c == DEC:
                                    a_, r_ = R0T[g][half[b], p, :], I64[b]
                                else:
                                    a_, r_ = (kkr[half[b], c, p, 0, :] if g == 0 else cht(kbe, c, p, b)), chain_of[g][half[b], c, p, :]
                                ins = pe.matmul(o, a_, r_, start=True, stop=(g == 1))
                                if g == 0:
                                    ins = pe.matmul(o, CD[half[b], c, p, 0, :], rVt[half[b], c, p, :], start=False, stop=True)
                        put(ins, ("rR_mm", "gR_mm")[g])
                    for g in range(2):
                        on(pe, layer, ("rR", "gR")[g], c + 1)
                        for p in range(2):
                            for b in range(2):
                                ins = pe.matmul(ps[half[b], 2 + g, p * 64:p * 64 + 64], Y[g][half[b], c * 2 + p],
                                                RR[g][half[b], c, p, :], start=True, stop=True)
                        put(ins, ("rU_mm", "gU_mm")[g])
                    if c == DEC:
                        break
                    for g in range(2):
                        on(pe, layer, ("rU", "gU")[g], c + 1)
                        for p in range(2):
                            for b in range(2):
                                o = ps[half[b], 6 + g, p * 64:p * 64 + 64]
                                if g == 0:
                                    pe.matmul(o, kLt[half[b], c, p, :], rVt[half[b], c, p, :], start=True, stop=False)
                                    ins = pe.matmul(o, bLt[half[b], c, p, :], UU[0][half[b], c, p, :], start=False, stop=True)
                                else:
                                    ins = pe.matmul(o, gkdt[half[b], c, p, :], UU[1][half[b], c, p, :], start=True, stop=True)
                        put(ins, ("rM_mm", "gM_mm")[g])

            def output(layer, g):
                if g == 0:
                    on(pe, layer, "rU")
                    on(pe, layer, "gU")
                    on(pe, layer, "rM")
                    on(pe, layer, "gM")
                if g == 2:
                    on(pe, layer, "lS")
                def f(c, p, b):
                    h = 2 * p + b
                    r = slice(DK * h, DK * h + DK)
                    o = ps[half[b], 2 * g + p, c * CH:(c + 1) * CH]
                    if g == 0:
                        rhs = kkr[half[b], c, p, 1, :]
                        terms = [(rVt[half[b], c, p, :], CD[half[b], c, p, 1, :]), (UU[0][half[b], c, p, :], BE[half[b], c, p, 1, :])]
                    elif g == 1:
                        rhs = cht(qe, c, p, b)
                        terms = [(UU[1][half[b], c, p, :], KQ[half[b], c, p, 1, :])]
                    else:
                        rhs = lqe[r, c * CH:(c + 1) * CH]
                        terms = [(lVt[half[b], c, p, :], At[half[b], p, c, :])]
                    if c < DEC:
                        pe.matmul(o, chain_of[g][half[b], c, p, :] if g < 2 else chain_l[r, c, :], rhs, start=True, stop=False)
                    else:
                        for q in range(DECB):
                            t = slice(q * DECT, (q + 1) * DECT)
                            pe.matmul(ps[half[b], 2 * g + p, TOK + q * DECT:TOK + (q + 1) * DECT],
                                      (Mrw, Mgdn)[g][half[b], p, 1 + q, :] if g < 2 else Mgla[r, 1 + q, :], rhs[:, t],
                                      start=True, stop=True)
                    for i, (l_, r_) in enumerate(terms):
                        ins = pe.matmul(o, l_, r_, start=(c == DEC and i == 0), stop=(i == len(terms) - 1))
                    return ins
                put(each(f), "out_mm")

            def head_mean(layer):
                on(pe, layer, "yo_dec", 1)
                for p in range(2):
                    ins = pe.matmul(ps[:, 6 + p, 0:TOK], C("hones"), yo[0][:, p, :], start=True, stop=True)
                put(ins, "mean_mm")

            def head_squares(layer, g):
                on(pe, layer, f"ysq{g}")
                on(pe, layer, "yo_dec", g + 1)
                for p in range(2):
                    ins = pe.matmul(ps[:, 2 * g + p, 0:TOK], C("hones"), ysq[g][:, p, :], start=True, stop=True)
                put(ins, "var_mm")

            def dec_states(layer, g):
                on(pe, layer, "VM", 2 * (g + 1))
                if g == 0:
                    on(pe, layer, "mean_read")
                else:
                    on(pe, layer, "yrs")
                b0 = DEC_BANK[g]
                for p in range(2):
                    for b in range(2):
                        h = 2 * p + b
                        r = slice(DK * h, DK * h + DK)
                        vm = VM[half[b], p].rearrange("q s v -> q (s v)")
                        um = UM[half[b], p].rearrange("q s v -> q (s v)")
                        o = ps[half[b], b0 + p, :]
                        if g == 0:
                            pe.matmul(o, kLt[half[b], DEC, p, :], vm, start=True, stop=False)
                            ins = pe.matmul(o, bLt[half[b], DEC, p, :], um, start=False, stop=True)
                        elif g == 1:
                            ins = pe.matmul(o, gkdt[half[b], DEC, p, :], um, start=True, stop=True)
                        else:
                            ins = pe.matmul(ps[r, b0, :], lkt[half[b], DEC, p, :], vm, start=True, stop=True)
                put(ins, "dec_mm")

            after_tile = {11: [lora], 15: [rw_sums], 19: [rw_products], 22: [rw_rows]}
            pe.wait_ge(const_in.sem, 32)
            with pe.Fori(0, DEPTH) as layer:
                ffn(layer, 0)
                first_tiles(layer, IN0, 1)
                for m in range(RING, IN_TILES):
                    on(pe, layer, in_read, m - 1 if m >= RING + 2 else m - 3)
                    tile_mm(layer, IN0 + m, m % 2)
                    for stage in after_tile.get(m, []):
                        stage(layer)
                inverse_t(layer, 0, 1)
                inverse_y(layer, 0, 1)
                inverse_t(layer, 0, 2)
                gdn_sums(layer)
                inverse_y(layer, 0, 2)
                gdn_bcast(layer)
                inverse_t(layer, 0, 3)
                gdn_products(layer)
                inverse_y(layer, 0, 3)
                gdn_rows(layer)
                gla_gate(layer)
                inverse_t(layer, 0, 4)
                gla_level(layer, 0)
                inverse_y(layer, 0, 4)
                inverse_t(layer, 1, 1)
                gla_level(layer, 1)
                inverse_t(layer, 0, 5)
                inverse_y(layer, 1, 1)
                gla_level(layer, 2)
                inverse_t(layer, 1, 2)
                inverse_y(layer, 0, 5)
                gla_level(layer, 3)
                inverse_y(layer, 1, 2)
                gla_level(layer, 4)
                inverse_t(layer, 1, 3)
                gla_level(layer, 5)
                inverse_y(layer, 1, 3)
                gla_level(layer, 6)
                inverse_t(layer, 1, 4)
                rg_gate(layer, 0)
                inverse_y(layer, 1, 4)
                rg_gate(layer, 1)
                inverse_t(layer, 1, 5)
                gla_rows(layer)
                inverse_y(layer, 1, 5)
                gla_states(layer)
                recurrences(layer)
                output(layer, 0)
                output(layer, 1)
                head_mean(layer)
                output(layer, 2)
                for g in range(3):
                    head_squares(layer, g)
                for g in range(3):
                    dec_states(layer, g)
                on(pe, layer, "o_lo", 4)
                for m in range(KT):
                    if m in DEC_BANK:
                        on(pe, layer, "dec_add", DEC_BANK.index(m) + 1)
                    tile_mm(layer, OUT0 + m, m)
                ffn(layer, 1)
            for k in range(KT):
                pe.wait_ge(sq_ready.sem, DEPTH * 24 + k + 1)
                ins = pe.matmul(ps[:, 7, 0:TOK], C("ones"), nsq[:, k, :], start=(k == 0), stop=(k == KT - 1))
            ins.then_inc(sum_mm.sem, 1)

        @block.scalar
        def _(act):
            def split_hi(layer, n, i=0):
                raw_landed(act, layer, n, i)
                slot_free(act, layer, n, i)
                act.activation(wh[:, n % RING, :], raw[:, n % RING, :], ACT.Copy).then_inc(hi_ready.sem, 1)

            def norm_split(layer, which, name):
                for k in range(KT):
                    if which:
                        act.wait_ge(x_new.sem, layer * 24 + (which - 1) * KT + k + 1)
                    act.activation(xh[:, k, :], x[:, k, :], ACT.Copy, scale=P(name, k)).then_inc(xh_ready.sem, 1)
                    act.activation(nsq[:, k, :], x[:, k, :], ACT.Square).then_inc(sq_ready.sem, 1)

            def rms(layer, which):
                act.wait_ge(sum_mm.sem, layer * 3 + which + 1)
                st(act.activation(lnt[:], ps[:, 7, 0:TOK], ACT.Ln, bias=C("e6"), scale=1.0 / D))
                st.settle()
                act.activation(rstd[:], lnt[:], ACT.Exp, scale=-0.5).then_inc(rstd_ready.sem, 1)

            def ffn(layer, f):
                base = f * FFN2

                def gate(m, i):
                    t = layer * 2 * FT + f * FT + i * 2 + m
                    split_hi(layer, base + RING + 2 * m, i)
                    act.wait_ge(gs_ready.sem, t + 1)
                    act.activation(gus[:, m, :], gus[:, m, :], ACT.Silu).then_inc(sil_ready.sem, 1)
                    split_hi(layer, base + RING + 2 * m + 1, i)
                    act.wait_ge(act_ready.sem, t + 1)
                    at = bass.ds(i * 2 + m, 1)
                    act.activation(hid_h[:, at, :].rearrange("q a t -> q (a t)"), gus[:, m, :], ACT.Copy).then_inc(hh_ready.sem, 1)

                with act.Fori(0, FT // 2) as i:
                    for m in range(2):
                        gate(m, i)
                splits(layer, base + 2 * FT + RING, min(FT, UNITS - RING - base - 2 * FT), split_hi, act)

            with act.Fori(0, DEPTH) as layer:
                st = Steps(act, a_step, layer, plain)

                def say(ins, name):
                    return st(ins, S[name])

                def fetch(dst, src, sem):
                    act.dma_start(dst, src[bass.ds(layer, 1), :, :].rearrange("a q n -> (a q) n")).then_inc(sem.sem, 16)

                fetch(pr[:], par, par_in)
                for n in range(RING):
                    split_hi(layer, n)
                act.wait_ge(const_in.sem, 32)
                act.wait_ge(par_in.sem, layer * 16 + 16)
                norm_split(layer, 0, "n1")
                rms(layer, 0)
                fetch(si[:], sin, state_in)
                fetch(ms[:], mst, state_in)
                ffn(layer, 0)
                norm_split(layer, 1, "nm")
                rms(layer, 1)
                for m in range(9):
                    split_hi(layer, IN0 + RING + m)
                on(act, layer, "xm")
                st(act.activation(xm[0:32, 6, :], xm[0:32, 6, :], ACT.Tanh))
                say(act.activation(xm[64:128, 6, :], xm[64:128, 6, :], ACT.Sigmoid), "lora_in")
                for m in range(9, 13):
                    split_hi(layer, IN0 + RING + m)
                on(act, layer, "lora_mm", 1)
                for p in range(2):
                    say(act.activation(sg[:, p, :], ps[:, 2 + p, 0:TOK], ACT.Sigmoid, bias=P("w0", p)), "sg")
                on(act, layer, "lora_mm", 2)
                on(act, layer, "shift_kept")
                for p in range(2):
                    say(act.activation(ra[:, p, :], ps[:, 4 + p, 0:TOK], ACT.Sigmoid, bias=P("a0", p)), "ra")
                on(act, layer, "lora_mm", 3)
                for p in range(2):
                    say(act.activation(rw_g[:, p, :], ps[:, 6 + p, 0:TOK], ACT.Copy), "rw_gc")
                for m in range(13, 17):
                    split_hi(layer, IN0 + RING + m)
                on(act, layer, "cum")
                st(act.activation(rP[:], cum[:], ACT.Exp, scale=-WDEC))
                st(act.activation(Pinv[:], cum[:], ACT.Exp, scale=WDEC))
                on(act, layer, "prev")
                say(act.activation(Pprev[:], sg[:], ACT.Exp, scale=-WDEC), "rw_P")
                on(act, layer, "kk_sum")
                for p in range(2):
                    st(act.activation(rsq[:, p, :], ps[:, 2 + p, 0:TOK], ACT.Ln, bias=C("e12")))
                st.settle()
                say(act.activation(rsq[:], rsq[:], ACT.Exp, scale=-0.5), "kk_rn")
                for m in range(17, 22):
                    split_hi(layer, IN0 + RING + m)
                on(act, layer, "rw_rows_mm", 1)
                st(act.activation(rVt[:].rearrange("q c p t -> q (c p) t"), banks(2, (0, 10)), ACT.Copy))
                on(act, layer, "rw_rows_mm", 2)
                st(act.activation(kLt[:].rearrange("q c p t -> q (c p) t"), banks(4, (0, 10)), ACT.Copy))
                on(act, layer, "rw_rows_mm", 3)
                say(act.activation(bLt[:].rearrange("q c p t -> q (c p) t"), banks(6, (0, 10)), ACT.Copy), "rw_rows")
                for m in range(22, 26):
                    split_hi(layer, IN0 + RING + m)
                def inverse_t(g, l):
                    on(act, layer, f"inv_mm{g}", 2 * l - 1)
                    say(act.activation(Tm[g][:, 0:blocks(l), :], banks(2 * g, (0, blocks(l))), ACT.Copy), f"T{g}")

                inverse_t(0, 1)
                on(act, layer, "conv")
                say(act.activation(cq[:], cq[:], ACT.Silu), "cq")
                on(act, layer, "cq")
                say(act.activation(gsq[:], cq[:, 0:4, :], ACT.Square), "gsq")
                R = slice(32, 32 + NH)
                say(act.activation(small[0:NH, :], small[0:NH, :], ACT.Sigmoid), "beta")
                st(act.activation(tiny[R, 10:11], P("alog")[R], ACT.Exp))
                st(act.activation(lnt[R, :], small[R, :], ACT.Abs, bias=P("dtb")[R]))
                st.settle()
                st(act.activation(lnt[R, :], lnt[R, :], ACT.Exp, scale=-1.0))
                st.settle()
                say(act.activation(lnt[R, :], lnt[R, :], ACT.Ln, bias=C("one")[R]), "sp_dt")
                inverse_t(0, 2)
                on(act, layer, "gdn_sum")
                for k in range(4):
                    st(act.activation(gsq[:, k, :], ps[:, 2 + k, 0:TOK], ACT.Ln, bias=C("e12")))
                st.settle()
                say(act.activation(gsq[:], gsq[:], ACT.Exp, scale=-0.5), "gdn_rn")
                on(act, layer, "Gb_mm")
                for p in range(2):
                    say(act.activation(Gb[:, p, :], ps[:, 6 + p, 0:TOK], ACT.Copy), "Gb")
                st.settle()
                say(act.activation(eG[:], Gb[:], ACT.Exp), "eG")
                on(act, layer, "Gdiff")
                say(act.activation(E[:], E[:], ACT.Exp), "E")
                on(act, layer, "Glast")
                say(act.activation(Gd[:], Gd[:], ACT.Exp), "eGd")
                inverse_t(0, 3)
                on(act, layer, "gdn_rows_mm", 1)
                st(act.activation(bvt[:].rearrange("q c p t -> q (c p) t"), banks(2, (0, 10)), ACT.Copy))
                on(act, layer, "gdn_rows_mm", 2)
                say(act.activation(gkdt[:].rearrange("q c p t -> q (c p) t"), banks(4, (0, 10)), ACT.Copy), "gdn_rows")
                on(act, layer, "gla_z")
                say(act.activation(ltm, ps[:, 7, 0:TOK], ACT.Abs, bias=P("gb")), "gla_ab")
                st.settle()
                st(act.activation(ltm, ltm, ACT.Exp, scale=-1.0))
                st.settle()
                say(act.activation(ltm, ltm, ACT.Ln, bias=C("one")), "gla_ln")
                def gla_scale(l):
                    n = TOK if l <= 3 else SEQ
                    on(act, layer, "lD", l)
                    st(act.activation(lE[:, 0:n], lE[:, 0:n], ACT.Abs))
                    st.settle()
                    say(act.activation(lE[:, 0:n], lE[:, 0:n], ACT.Exp, scale=-1.0 / GLA_TAU), "lE")

                inverse_t(0, 4)
                gla_scale(1)
                gla_scale(2)
                inverse_t(1, 1)
                inverse_t(0, 5)
                gla_scale(3)
                inverse_t(1, 2)
                gla_scale(4)
                gla_scale(5)
                inverse_t(1, 3)
                gla_scale(6)
                on(act, layer, "lBl")
                st(act.activation(lkd, lkd, ACT.Exp, scale=1.0 / GLA_TAU))
                say(act.activation(lB, lB, ACT.Exp, scale=1.0 / GLA_TAU), "leB")
                st(act.activation(tiny[:, 11:13], P("lam", 0, 2), ACT.Abs))
                st.settle()
                st(act.activation(tiny[:, 11:13], tiny[:, 11:13], ACT.Exp, scale=-1.0))
                st.settle()
                say(act.activation(tiny[:, 11:13], tiny[:, 11:13], ACT.Ln, bias=C("one")), "sp_lam")
                inverse_t(1, 4)
                on(act, layer, "rg_mm", 1)
                for p in range(2):
                    say(act.activation(rr[:, p, :], ps[:, 6 + p, 0:TOK], ACT.Sigmoid, bias=P("ba", p)), "rg_gates")
                on(act, layer, "rg_mm", 2)
                for p in range(2):
                    say(act.activation(ri[:, p, :], ps[:, 6 + p, 0:TOK], ACT.Sigmoid, bias=P("bx", p)), "rg_gates")
                inverse_t(1, 5)
                st(act.activation(gz[:], gz[:], ACT.Silu))
                st(act.activation(gt[:], gt[:], ACT.Silu))
                say(act.activation(rgg[:], rgg[:], ACT.Gelu_apprx_tanh), "gates")
                on(act, layer, "gla_rows_mm", 1)
                st(act.activation(lkt[:].rearrange("q c p t -> q p c t"),
                                  ps[:, 6:8, 0:NC * DK].rearrange("q p (c t) -> q p c t", c=NC), ACT.Copy))
                on(act, layer, "gla_rows_mm", 2)
                say(act.activation(lVt[:].rearrange("q c p t -> q (c p) t"), banks(4, (0, 10)), ACT.Copy), "gla_rows")
                on(act, layer, "rg_y")
                on(act, layer, "rgc_kept")
                st(act.activation(rgt[:], rr[:], ACT.Tanh))
                say(act.activation(rga[:], rr[:], ACT.Exp, scale=-1.0), "rg_a")
                on(act, layer, "rg_b2")
                say(act.activation(rgb[:], rgt[:], ACT.Sqrt), "rg_b")
                on(act, layer, "o_ready", 1)
                say(act.activation(xh[:, 2:4, :], rr[:], ACT.Copy), "o_hi")
                for g in range(2):
                    on(act, layer, "R0_mm", g + 1)
                    say(act.activation(R0T[g], ps[:, 4 + g, 0:128].rearrange("q (p t) -> q p t", p=2), ACT.Copy), "R0T")
                for c in range(NC):
                    on(act, layer, "rR_mm", c + 1)
                    say(act.activation(RR[0][:, c], ps[:, 0, 0:128].rearrange("q (p t) -> q p t", p=2), ACT.Copy), "rR")
                    on(act, layer, "rU_mm", c + 1)
                    say(act.activation(UU[0][:, c], ps[:, 2, 0:128].rearrange("q (p t) -> q p t", p=2), ACT.Copy, scale=-1.0), "rU")
                def take_out(g):
                    on(act, layer, "out_mm", g + 1)
                    say(act.activation(yo[g][:], ps[:, 2 * g:2 * g + 2, 0:TOK], ACT.Copy), "yo")

                def square(g):
                    say(act.activation(ysq[g][:], yo[g][:], ACT.Square), f"ysq{g}")

                take_out(0)
                take_out(1)
                on(act, layer, "yo_dec", 2)
                square(1)
                on(act, layer, "mean_read")
                square(0)
                take_out(2)
                on(act, layer, "yo_dec", 3)
                square(2)
                on(act, layer, "var_mm", 1)
                st(act.activation(ysq[0][:], ps[:, 0:2, 0:TOK], ACT.Ln, bias=C("gne"), scale=1.0 / HD))
                on(act, layer, "var_mm", 3)
                st(act.activation(ysq_12[:], ps[:, 2:6, 0:TOK], ACT.Ln, bias=C("e6"), scale=1.0 / HD))
                st.settle()
                say(act.activation(ysq[0][:], ysq[0][:], ACT.Exp, scale=-0.5), "yrs")
                say(act.activation(ysq_12[:], ysq_12[:], ACT.Exp, scale=-0.5), "yrs")
                for g, k0 in ((0, 0), (1, 4), (2, 6)):
                    on(act, layer, "o_ready", g + 2)
                    say(act.activation(xh[:, k0:k0 + 2, :], yo[g][:], ACT.Copy), "o_hi")
                for m in range(26, 26 + KT):
                    split_hi(layer, IN0 + RING + m)
                for name in ("shift_kept", "gc_kept", "rgc_kept", "rg_kept"):
                    on(act, layer, name)
                act.dma_start(sout[bass.ds(layer, 1), :, :].rearrange("a q n -> (a q) n"), so[:]).then_inc(state_out.sem, 16)
                on(act, layer, "dec_add")
                for name in ("rM", "gM", "lS"):
                    on(act, layer, name)
                act.dma_start(mout[bass.ds(layer, 1), :, :].rearrange("a q n -> (a q) n"), ms[:]).then_inc(state_out.sem, 16)
                norm_split(layer, 2, "n2")
                rms(layer, 2)
                ffn(layer, 1)
                on(act, layer, x_new)
                on(act, layer, xl_ready)
                act.wait_ge(state_out.sem, layer * 32 + 32)
            for k in range(KT):
                act.activation(nsq[:, k, :], x[:, k, :], ACT.Square).then_inc(sq_ready.sem, 1)
            act.wait_ge(sum_mm.sem, DEPTH * 3 + 1)
            act.activation(lnt[:], ps[:, 7, 0:TOK], ACT.Ln, bias=C("e6"), scale=1.0 / D).then_inc(a_step.sem, 1)
            act.wait_ge(a_step.sem, DEPTH * A_STEPS + 1)
            act.activation(rstd[:], lnt[:], ACT.Exp, scale=-0.5).then_inc(rstd_ready.sem, 1)
            act.wait_ge(state_out.sem, DEPTH * 32)

        @block.vector
        def _(ve):
            tt, ts, stt = ve.tensor_tensor, ve.tensor_scalar, ve.scalar_tensor_tensor

            def split_lo(layer, n, i=0):
                ve.wait_ge(hi_ready.sem, layer * UNITS + i * RING + n + 1)
                s = n % RING
                tt(wl[:, s, :], raw[:, s, :], wh[:, s, :].bitcast(F32), ALU.subtract).then_inc(lo_ready.sem, 1)

            def norm_low(layer, which, name, scale=None):
                def add(k):
                    stt(x[:, k, :], ps[:, k, 0:TOK], scale, x[:, k, :], ALU.mult, ALU.add).then_inc(x_new.sem, 1)

                ahead = RING
                if which:
                    for k in range(ahead):
                        add(k)
                for k in range(KT):
                    ve.wait_ge(xh_ready.sem, layer * 24 + which * KT + k + 1)
                    stt(xl[:, k, :], x[:, k, :], P(name, k), xh[:, k, :].bitcast(F32), ALU.mult, ALU.subtract).then_inc(xl_ready.sem, 1)
                    if which and k + ahead < KT:
                        add(k + ahead)

            def ffn(layer, f):
                base = f * FFN2
                apart(ve, rstd_ready, rstd_ready.upto(layer, 2 * f + 1))

                def gate(m, i):
                    t = layer * 2 * FT + f * FT + i * 2 + m
                    ve.wait_ge(unit_used.sem, layer * UNITS + i * RING + base + 2 * m + 2)
                    tt(gus[:, m, :], ps[:, 2 * m, 0:TOK], rstd[:], ALU.mult).then_inc(gs_ready.sem, 1)
                    tt(gus[:, 2 + m, :], ps[:, 2 * m + 1, 0:TOK], rstd[:], ALU.mult).then_inc(gu_read.sem, 1)
                    split_lo(layer, base + RING + 2 * m, i)
                    ve.wait_ge(sil_ready.sem, t + 1)
                    ve.wait_ge(gu_read.sem, t + 1)
                    tt(gus[:, m, :], gus[:, m, :], gus[:, 2 + m, :], ALU.mult).then_inc(act_ready.sem, 1)
                    split_lo(layer, base + RING + 2 * m + 1, i)
                    ve.wait_ge(hh_ready.sem, t + 1)
                    at = bass.ds(i * 2 + m, 1)
                    tt(hid_l[:, at, :].rearrange("q a t -> q (a t)"), gus[:, m, :],
                       hid_h[:, at, :].rearrange("q a t -> q (a t)").bitcast(F32), ALU.subtract).then_inc(hl_ready.sem, 1)

                with ve.Fori(0, FT // 2) as i:
                    for m in range(2):
                        gate(m, i)
                splits(layer, base + 2 * FT + RING, min(FT, UNITS - RING - base - 2 * FT), split_lo, ve)
                ve.wait_ge(unit_used.sem, layer * UNITS + base + FFN_UNITS)

            with ve.Fori(0, DEPTH) as layer:
                st = Steps(ve, v_step, layer, plain)

                def say(ins, name):
                    return st(ins, S[name])

                def evac(m):
                    ve.wait_ge(unit_used.sem, layer * UNITS + IN0 + m + 1)
                    src = ps[:, m if m < RING else m % 2, 0:TOK]
                    padded = {T_RW: (rwp, 1), T_GDN: (gcp, 3), T_RG: (rgp, 3)}
                    for t0, n in ((T_RW, 7), (T_GDN, 6), (T_RG, 2)):
                        if t0 <= m < t0 + n:
                            buf, pad = padded[t0]
                            st(tt(buf[:, m - t0, pad:pad + SEQ], src[:, 0:SEQ], rstd[:, 0:SEQ], ALU.mult))
                            st(tt(seqs(buf[:, m - t0, :], pad, pad), src[:, SEQ:].rearrange("q (s t) -> q s t", s=DECB),
                                  rstd[:, SEQ:].rearrange("q (s t) -> q s t", s=DECB), ALU.mult), in_read)
                            break
                    else:
                        dst = small if m == T_SMALL else gz[:, m - T_Z, :] if T_Z <= m < T_GLA else \
                            gla[:, m - T_GLA, :] if m < T_GT else gt[:, m - T_GT, :] if m < T_RG else rgg[:, m - T_RGG, :]
                        st(tt(dst, src, rstd[:], ALU.mult), in_read)
                    split_lo(layer, IN0 + RING + m)

                def rw_mix():
                    on(ve, layer, "pads")
                    st.settle()
                    st(tt(xm[:, :, 0:SEQ], rwp[:, :, 0:SEQ], rwp[:, :, 1:1 + SEQ], ALU.subtract))
                    st(tt(seqs(xm, 0), seqs(rwp, 1, 0), seqs(rwp, 1, 1), ALU.subtract))
                    st.settle()
                    for k in range(7):
                        st(stt(xm[:, k, 0:SEQ], xm[:, k, 0:SEQ], P("mu", k), rwp[:, k, 1:1 + SEQ], ALU.mult, ALU.add))
                        say(stt(seqs(xm[:, k, :], 0), seqs(xm[:, k, :], 0), P("mu", k), seqs(rwp[:, k, :], 1, 1), ALU.mult, ALU.add), "xm")
                    st.settle()

                def rw_keys():
                    on(ve, layer, "shift_kept")
                    for p in range(2):
                        say(ts(kk[:, p, :], xm[:, 2 + p, :], P("kk", p), None, ALU.mult), "kkraw")
                    st(ts(tiny[:, 13:15], P("ka", 0, 2), -1.0, 1.0, ALU.mult, ALU.add))
                    on(ve, layer, "ra")
                    st.settle()
                    for p in range(2):
                        st(ts(kmod[:, p, :], ra[:, p, :], P("ka", p), tiny[:, 13 + p:14 + p], ALU.mult, ALU.add))
                    st.settle()
                    st(tt(kmod[:], kmod[:], xm[:, 2:4, :], ALU.mult))
                    st.settle()
                    for p in range(2):
                        say(stt(rtm[:, p, :], xm[:, p, :], P("rk", p), kmod[:, p, :], ALU.mult, ALU.mult), "rkr")

                def rw_decay():
                    on(ve, layer, "sg")
                    for p in range(2):
                        say(ve.tensor_tensor_scan(cum[:, p, :], C("cmask"), sg[:, p, :], 0.0, ALU.mult, ALU.add), "cum")
                    on(ve, layer, "cum")
                    say(tt(sg[:], cum[:], sg[:], ALU.subtract), "prev")

                def rw_scaled():
                    on(ve, layer, "kk_rn")
                    st(tt(kk[:], kk[:], rsq[:], ALU.mult))
                    st.settle()
                    say(tt(ra[:], kk[:], ra[:], ALU.mult), "rb")
                    on(ve, layer, "rw_P")
                    st(tt(kkr[:, :, :, 0, :], chunked(kk), chunked(Pprev), ALU.mult))
                    say(tt(kkr[:, :, :, 1, :], chunked(xm[:, 0:2, :]), chunked(rP), ALU.mult), "rw_ops")
                    say(tt(kPi[:], kmod[:], Pinv[:], ALU.mult), "kPi")
                    on(ve, layer, "rk_sum")
                    say(tt(rw_bonus[:], ps[:, 4:6, 0:TOK], xm[:, 4:6, :], ALU.mult), "bonus")

                def rw_masks():
                    for g, (src_banks, dst) in enumerate((((2, 3, 6), BE), ((4, 5, 7), CD))):
                        on(ve, layer, "rw_pairs", g + 1)
                        for j, bank in enumerate(src_banks):
                            n = 4 if j < 2 else 2
                            say(tt(dst[:, 2 * j:2 * j + n // 2].rearrange("q c p k t -> q (c p) (k t)"),
                                   ps[:, bank, 0:n * 128].rearrange("q (u t) -> q u t", u=n),
                                   tri[:, j // 2].rearrange("q k t -> q (k t)").unsqueeze(1).broadcast_to([128, n, 128]),
                                   ALU.mult), "rw_pairs_read")

                def conv(dst, src, tiles, w, name, bias=None, these=None):
                    for k in range(CONV):
                        if k:
                            st.settle()
                        for j in these or range(tiles):
                            wk = P(w, tiles * k + j)
                            for d_, s_, last_ in ((dst[:, j, 0:SEQ], src[:, j, k:k + SEQ], False),
                                                  (seqs(dst[:, j, :], 0), seqs(src[:, j, :], 3, k), True)):
                                if k == 0 and bias:
                                    ins = ts(d_, s_, wk, P(bias, j), ALU.mult, ALU.add)
                                elif k == 0:
                                    ins = ts(d_, s_, wk, None, ALU.mult)
                                else:
                                    ins = stt(d_, s_, wk, d_, ALU.mult, ALU.add)
                                say(ins, name) if last_ and k == CONV - 1 else st(ins)

                def gdn_conv(*these):
                    on(ve, layer, "kk_sum")
                    on(ve, layer, "rk_sum")
                    on(ve, layer, "bPi")
                    st.settle()
                    conv(cq, gcp, 6, "gcw", "conv", these=these)

                def gdn_gate():
                    R = slice(32, 32 + NH)
                    on(ve, layer, "sp_dt")
                    st(ts(small[R, :], small[R, :], P("dtb")[R], 0.0, ALU.add, ALU.max))
                    st.settle()
                    st(tt(small[R, :], small[R, :], lnt[R, :], ALU.add))
                    st.settle()
                    st(ts(lnt[R, :], small[R, :], tiny[R, 10:11], -1.0, ALU.mult, ALU.mult))
                    st.settle()
                    say(ve.tensor_tensor_scan(small[R, :], C("cmask")[R, :], lnt[R, :], 0.0, ALU.mult, ALU.add), "gcum")

                def last_minus(dst, v, two):
                    pv = v[:, :, 0:SEQ].rearrange("q p (c t) -> q p c t", c=DEC) if two else v[:, 0:SEQ].rearrange("q (c t) -> q c t", c=DEC)
                    dv = seqs(v, 0)
                    pd = dst[:, :, 0:SEQ].rearrange("q p (c t) -> q p c t", c=DEC) if two else dst[:, 0:SEQ].rearrange("q (c t) -> q c t", c=DEC)
                    dd = seqs(dst, 0)
                    yield tt(pd, pv[..., CH - 1:CH].broadcast_to(list(pv.shape)), pv, ALU.subtract)
                    yield tt(dd, dv[..., DECT - 1:DECT].broadcast_to(list(dv.shape)), dv, ALU.subtract)

                def gdn_keys():
                    on(ve, layer, "gdn_rn")
                    on(ve, layer, "cq")
                    say(stt(cq[:, 0:2, :], cq[:, 0:2, :], HD ** -0.5, gsq[:, 0:2, :], ALU.mult, ALU.mult), "gq")
                    st(tt(cq[:, 2:4, :], cq[:, 2:4, :], gsq[:, 2:4, :], ALU.mult))
                    on(ve, layer, "bb_mm")
                    st.settle()
                    on(ve, layer, "gc_kept")
                    on(ve, layer, "rw_rows_mm", 3)
                    say(tt(kq[:, :, :, 0, :], chunked(cq[:, 2:4, :]), ps[:, 2:4, 0:TOK].rearrange("q p (c t) -> q c p t", c=NC), ALU.mult), "kq")
                    say(tt(vb[:], cq[:, 4:6, :], ps[:, 2:4, 0:TOK], ALU.mult), "vb")
                    on(ve, layer, "Gc_mm")
                    say(ve.tensor_copy(Gc, ps[:, 4, 0:10].rearrange("q (c p) -> q c p", c=NC)), "Gc")
                    on(ve, layer, "Gb")
                    on(ve, layer, "Gc")
                    st(tt(E[:], chunked(Gb), Gc.unsqueeze(3).broadcast_to([128, NC, 2, CH]), ALU.subtract))
                    st.settle()
                    say(ts(E[:], E[:], 0.0, None, ALU.min), "Gdiff")
                    gl = list(last_minus(Gd, Gb, True))
                    st(gl[0]); say(gl[1], "Glast")
                    on(ve, layer, "eG")
                    on(ve, layer, "kq")
                    st(tt(chunked(kbe), kq[:, :, :, 0, :], chunked(eG), ALU.mult))
                    st(tt(qe[:], cq[:, 0:2, :], eG[:], ALU.mult))
                    on(ve, layer, "eGd")
                    say(tt(kd[:], cq[:, 2:4, :], Gd[:], ALU.mult), "kd")

                def gdn_pairs():
                    on(ve, layer, "KQ_mm")
                    on(ve, layer, "EM")
                    for j, bank in enumerate((5, 6, 7)):
                        n = 4 if j < 2 else 2
                        say(tt(KQ[:, 2 * j:2 * j + n // 2].rearrange("q c p k t -> q (c p) (k t)"),
                               ps[:, bank, 0:n * 128].rearrange("q (u t) -> q u t", u=n),
                               EM[:, 2 * j:2 * j + n // 2].rearrange("q c p k t -> q (c p) (k t)"), ALU.mult), "KQ")

                def gla_decay():
                    on(ve, layer, "KQ")
                    on(ve, layer, "gdn_rows")
                    on(ve, layer, "gla_ab")
                    say(ts(gla[:, 0, :], gla[:, 0, :], DK ** -0.5, None, ALU.mult), "gla_q")
                    say(ts(lE, ps[:, 7, 0:TOK], P("gb"), 0.0, ALU.add, ALU.min), "gla_min")
                    on(ve, layer, "gla_ln")
                    st.settle()
                    st(tt(lE, lE, ltm, ALU.subtract))
                    st.settle()
                    st(ve.tensor_tensor_scan(lB, C("cmask"), lE, 0.0, ALU.mult, ALU.add))
                    st.settle()
                    on(ve, layer, "At_zero")

                def take(l):
                    nch = NC if l <= 3 else DEC
                    if l:
                        st.settle()
                    apart(ve, S["gla_lev"], S["gla_lev"].upto(layer, l + 1))
                    for p in range(2):
                        say(ve.copy_predicated(At[:, p, 0:nch, :], lev[:, l, :].bitcast(U32).unsqueeze(1).broadcast_to([128, nch, CH]),
                                               ps[:, 4 + p, 0:nch * CH].rearrange("q (c t) -> q c t", c=nch)), "gla_take")

                def gla_scale(l):
                    s, n = 1 << (l - 1), (TOK if l <= 3 else SEQ)
                    v = lB[:, 0:n].rearrange("q (g t) -> q g t", t=2 * s)
                    if l >= 2:
                        on(ve, layer, "lks", l - 1)
                        on(ve, layer, "lqs", l - 1)
                    say(tt(lE[:, 0:n].rearrange("q (g t) -> q g t", t=2 * s), v, v[:, :, s - 1:s].broadcast_to(list(v.shape)), ALU.subtract), "lD")
                    on(ve, layer, "lE", l)
                    if l >= 3:
                        on(ve, layer, "gla_lev", l - 1)
                    say(tt(lqs[l % 2][:, 0:n], gla[:, 0, 0:n], lE[:, 0:n], ALU.mult), "lqs")

                def gla_last():
                    gl = list(last_minus(lkd, lB, False))
                    st(gl[0]); say(gl[1], "lBl")
                    on(ve, layer, "leB")
                    st(tt(lqe, gla[:, 0, :], lB, ALU.mult))
                    say(tt(lkd, gla[:, 1, :], lkd, ALU.mult), "lkd")

                def gla_chain():
                    on(ve, layer, "lS_mm")
                    on(ve, layer, "chain_zero")
                    ve.wait_ge(state_in.sem, layer * 32 + 32)
                    for c in range(DEC):
                        dst = chain_l[:, c + 1, :] if c + 1 < DEC else Mgla[:, 0, :]
                        say(stt(dst, chain_l[:, c, :], lB[:, c * CH + CH - 1:c * CH + CH], ps[:, 6, c * 64:c * 64 + 64],
                                ALU.mult, ALU.add), "lS")
                        st.settle()

                def rg_conv():
                    on(ve, layer, "KQ_mm")
                    conv(xc, rgp, 2, "rgcw", "xc", "rgcb")

                def rg_steps():
                    st(ts(tiny[:, 13:15], P("lam", 0, 2), -1.0, 0.0, ALU.mult, ALU.max))
                    on(ve, layer, "sp_lam")
                    st.settle()
                    st(tt(tiny[:, 13:15], tiny[:, 13:15], tiny[:, 11:13], ALU.add))
                    st.settle()
                    on(ve, layer, "rg_gates")
                    st(tt(ri[:], ri[:], xc[:], ALU.mult))
                    for p in range(2):
                        say(ts(rr[:, p, :], rr[:, p, :], tiny[:, 13 + p:14 + p], 8.0, ALU.mult, ALU.mult), "rg_y")

                def rg_scan():
                    on(ve, layer, "rg_a")
                    st(tt(rgb[:], rga[:], rga[:], ALU.mult))
                    st.settle()
                    st(ts(rgb[:], rgb[:], 1.0, None, ALU.add))
                    st.settle()
                    say(stt(rgt[:], rgt[:], 1e-34, rgb[:], ALU.max, ALU.mult), "rg_b2")
                    on(ve, layer, "rg_b")
                    st.settle()
                    st(tt(rgb[:], rgb[:], ri[:], ALU.mult))
                    ve.wait_ge(state_in.sem, layer * 32 + 32)
                    h0 = io(si, SIN, "h", "q (p s) -> q p s", p=2)
                    st(tt(rgt[:, :, 0:DECB], seqs(rga, 0, 0, 1).rearrange("q p s t -> q p (s t)"), h0, ALU.mult))
                    st.settle()
                    first = seqs(rgb, 0, 0, 1).rearrange("q p s t -> q p (s t)")
                    st(tt(first, first, rgt[:, :, 0:DECB], ALU.add))
                    st(ve.memset(rga[:, :, 0:1], 0.0))
                    st(ve.memset(seqs(rga, 0, 0, 1), 0.0))
                    st.settle()
                    for p in range(2):
                        say(ve.tensor_tensor_scan(ri[:, p, :], rga[:, p, :], rgb[:, p, :], 0.0, ALU.mult, ALU.add), "rg_h")
                    st.settle()
                    on(ve, layer, "gates")
                    say(tt(rr[:], ri[:], rgg[:], ALU.mult), "o_ready")

                def o_low(k, src, g):
                    on(ve, layer, "o_hi", g)
                    say(tt(xl[:, k:k + 2, :], src, xh[:, k:k + 2, :].bitcast(F32), ALU.subtract), "o_lo")

                def turn(g, n):
                    st.settle()
                    say(ve.transpose(X[g][:, 0:n, :].rearrange("q m s -> q (m s)"), Y[g][:, 0:n, :].rearrange("q m s -> q (m s)")),
                        f"XY{g}")

                def inverse(g, l):
                    y_ = Y[g][:, 0:blocks(l), :]
                    if l == 0:
                        on(ve, layer, f"LB{g}", 1)
                        eye = lev[:, 0, :].unsqueeze(1).broadcast_to([128, 10, CH])
                        say(tt(y_, eye, LB[g][:], ALU.subtract), f"XY{g}")
                    else:
                        on(ve, layer, f"inv_mm{g}", 2 * l)
                        say(tt(y_, y_, banks(2 * g, (0, blocks(l))), ALU.subtract), f"XY{g}")
                    if l < 5:
                        turn(g, blocks(l))

                def recurrences():
                    for c in range(NC):
                        on(ve, layer, "gR_mm", c + 1)
                        say(tt(RR[1][:, c], bvt[:, c], ps[:, 1, 0:128].rearrange("q (p t) -> q p t", p=2), ALU.subtract), "gR")
                        on(ve, layer, "gU_mm", c + 1)
                        say(ve.tensor_copy(UU[1][:, c], ps[:, 3, 0:128].rearrange("q (p t) -> q p t", p=2)), "gU")
                        if c == DEC:
                            break
                        t = c * CH + CH - 1
                        for g, (M, D_) in enumerate(((Mrw, rP), (Mgdn, eG))):
                            on(ve, layer, ("rM_mm", "gM_mm")[g], c + 1)
                            for p in range(2):
                                dst = chain_of[g][:, c + 1, p, :] if c + 1 < DEC else M[:, p, 0, :]
                                say(stt(dst, chain_of[g][:, c, p, :], D_[:, p, t:t + 1], ps[:, 6 + g, p * 64:p * 64 + 64], ALU.mult, ALU.add),
                                    ("rM", "gM")[g])
                        st.settle()

                def add_dec(g):
                    on(ve, layer, "yo", g + 1)
                    d_ = yo[g][:, :, SEQ:]
                    say(tt(d_, d_, ps[:, 2 * g:2 * g + 2, TOK:TOK + CH], ALU.add), "yo_dec")

                def center():
                    on(ve, layer, "mean_mm")
                    say(stt(yo[0][:], ps[:, 6:8, 0:TOK], -1.0 / HD, yo[0][:], ALU.mult, ALU.add), "mean_read")

                def finish(g):
                    y = yo[g]
                    on(ve, layer, "yrs", min(g, 1) + 1)
                    st(tt(y[:], y[:], ysq[g][:], ALU.mult))
                    st.settle()
                    if g == 0:
                        for p in range(2):
                            st(ts(y[:, p, :], y[:, p, :], P("lnw", p), P("lnb", p), ALU.mult, ALU.add))
                        st.settle()
                        st(tt(y[:], y[:], rw_bonus[:], ALU.add))
                        st.settle()
                        say(tt(y[:], y[:], rw_g[:], ALU.mult), "o_ready")
                    else:
                        say(stt(y[:], y[:], P("gnw" if g == 1 else "glw"), (gz if g == 1 else gt)[:], ALU.mult, ALU.mult), "o_ready")

                def dec_add(g):
                    on(ve, layer, "dec_mm", g + 1)
                    on(ve, layer, "dec_decay", g + 1)
                    b0 = DEC_BANK[g]
                    if g < 2:
                        M = (Mrw, Mgdn)[g]
                        v = M[:, :, 1:, :].rearrange("q p s v -> q p (s v)")
                        say(tt(v, v, ps[:, b0:b0 + 2, :], ALU.add), "dec_add")
                    else:
                        v = Mgla[:, 1:, :].rearrange("q s v -> q (s v)")
                        say(tt(v, v, ps[:, b0, :], ALU.add), "dec_add")

                for n in range(RING):
                    split_lo(layer, n)
                ve.wait_ge(const_in.sem, 32)
                norm_low(layer, 0, "n1")
                ffn(layer, 0)
                norm_low(layer, 1, "nm", 0.5)
                on(ve, layer, rstd_ready, 2)
                ve.wait_ge(unit_used.sem, layer * UNITS + IN0)
                work = {8: [rw_mix], 12: [rw_decay], 13: [rw_keys], 16: [rw_scaled], 20: [rw_masks],
                        21: [lambda: gdn_conv(0, 1)], 22: [lambda: gdn_conv(2)], 23: [lambda: gdn_conv(3)],
                        24: [lambda: gdn_conv(4)], 25: [lambda: inverse(0, 0), lambda: gdn_conv(5)]}
                for m in range(IN_TILES):
                    evac(m)
                    for stage in work.get(m, []):
                        stage()
                inverse(0, 1)
                gdn_gate()
                inverse(0, 2)
                gdn_keys()
                gdn_pairs()
                inverse(0, 3)
                gla_decay()
                inverse(1, 0)
                gla_scale(1)
                take(0)
                inverse(0, 4)
                gla_scale(2)
                take(1)
                inverse(1, 1)
                gla_scale(3)
                take(2)
                inverse(0, 5)
                gla_scale(4)
                take(3)
                inverse(1, 2)
                gla_scale(5)
                take(4)
                rg_conv()
                gla_scale(6)
                take(5)
                inverse(1, 3)
                take(6)
                gla_last()
                inverse(1, 4)
                rg_steps()
                inverse(1, 5)
                gla_chain()
                rg_scan()
                o_low(2, rr[:], 1)
                recurrences()
                add_dec(0)
                add_dec(1)
                center()
                add_dec(2)
                finish(0)
                finish(1)
                o_low(0, yo[0][:], 2)
                finish(2)
                o_low(4, yo[1][:], 3)
                o_low(6, yo[2][:], 4)
                for g in range(3):
                    dec_add(g)
                for m in range(IN_TILES, IN_TILES + KT):
                    split_lo(layer, IN0 + RING + m)
                ve.wait_ge(unit_used.sem, layer * UNITS + FFN2)
                norm_low(layer, 2, "n2", 1.0)
                ffn(layer, 1)
                for k in range(KT):
                    stt(x[:, k, :], ps[:, k, 0:TOK], 0.5, x[:, k, :], ALU.mult, ALU.add).then_inc(x_new.sem, 1)
            ve.wait_ge(rstd_ready.sem, DEPTH * 3 + 1)
            for k in range(KT):
                stt(x[:, k, :], x[:, k, :], C("nf", k, 1), rstd[:], ALU.mult, ALU.mult).then_inc(x_new.sem, 1)

        @block.gpsimd
        def _(gp):
            with gp.Fori(0, DEPTH) as layer:
                st = Steps(gp, g_step, layer, apart)


                def say(ins, name):
                    return st(ins, S[name])

                def kept(buf, pad, name, dims):
                    n = pad
                    out = so[:, SOUT[name][0]:SOUT[name][0] + SOUT[name][1]].rearrange("q (k s t) -> q k s t", k=dims, s=NSEQ)
                    st(gp.tensor_copy(out[:, :, 0, :], buf[:, :, SEQ:SEQ + pad]))
                    return gp.tensor_copy(out[:, :, 1:, :], seqs(buf, pad, DECT, pad))

                on(gp, layer, rstd_ready, 2)
                apart(gp, state_in, layer * 32 + 32)
                for buf, pad, name, dims in ((rwp, 1, "shift", 7), (gcp, 3, "gc", 6), (rgp, 3, "rgc", 2)):
                    st(gp.memset(buf[:, :, 0:pad], 0.0))
                    src = si[:, SIN[name][0]:SIN[name][0] + SIN[name][1]].rearrange("q (k s t) -> q k s t", k=dims, s=DECB)
                    ins = gp.tensor_copy(seqs(buf, pad, 0, pad), src)
                    say(ins, "pads") if dims == 2 else st(ins)
                say(gp.memset(chain[:], 0.0), "chain_zero")
                on(gp, layer, in_read, 7)
                say(kept(rwp, 1, "shift", 7), "shift_kept")
                on(gp, layer, "kkraw")
                on(gp, layer, "xm")
                say(gp.tensor_tensor(rsq[:], kk[:], kk[:], ALU.mult), "kk_sq")
                on(gp, layer, "rb")
                on(gp, layer, "rw_P")
                say(gp.tensor_tensor(bPi[:], ra[:], Pinv[:], ALU.mult), "bPi")
                st.settle()
                on(gp, layer, "kPi")
                for dst, src in ((kL, kPi), (bL, bPi)):
                    for p in range(2):
                        pe_ = rP[:, p, 0:SEQ].rearrange("q (c t) -> q c t", c=DEC)[:, :, CH - 1:CH].broadcast_to([128, DEC, CH])
                        st(gp.tensor_tensor(dst[:, p, 0:SEQ].rearrange("q (c t) -> q c t", c=DEC),
                                            src[:, p, 0:SEQ].rearrange("q (c t) -> q c t", c=DEC), pe_, ALU.mult))
                        de_ = seqs(rP[:, p, :], 0)[:, :, DECT - 1:DECT].broadcast_to([128, DECB, DECT])
                        say(gp.tensor_tensor(seqs(dst[:, p, :], 0), seqs(src[:, p, :], 0), de_, ALU.mult), "kbL")
                on(gp, layer, in_read, T_SMALL)
                say(kept(gcp, 3, "gc", 6), "gc_kept")

                def gla_keys(l):
                    n = TOK if l <= 3 else SEQ
                    on(gp, layer, "lE", l)
                    if l >= 3:
                        on(gp, layer, "gla_lev", l - 1)
                    say(gp.tensor_tensor(lks[l % 2][:, 0:n], gla[:, 1, 0:n], lE[:, 0:n], ALU.mult), "lks")

                def blocks_below(g, l):
                    nu = blocks(l)
                    m_ = lev[:, l + 1, :].unsqueeze(1).broadcast_to([128, nu, CH])
                    if l == 1:
                        on(gp, layer, f"XY{g}", 1)
                    elif l > 1:
                        on(gp, layer, f"inv_mm{g}", 2 * l - 3)
                    s_ = (BE, KQ)[g][:].rearrange("q c p k t -> q (c p) k t")[:, 0:nu, 0, :]
                    say(gp.tensor_tensor(LB[g][:, 0:nu, :], s_, m_, ALU.mult), f"LB{g}")

                on(gp, layer, "rw_pairs_read", 3)
                blocks_below(0, 0)
                blocks_below(0, 1)
                blocks_below(0, 2)
                on(gp, layer, "gq")
                say(gp.tensor_copy(kq[:, :, :, 1, :], chunked(cq[:, 0:2, :])), "kq_q")
                blocks_below(0, 3)
                on(gp, layer, "E")
                for k, (lo, n) in enumerate(((0, 8), (8, 2))):
                    for j in range(2):
                        e_ = E[:].rearrange("q c p t -> q (c p) t")[:, lo:lo + n, :]
                        m_ = tri[:, k, j, :].unsqueeze(1).broadcast_to([128, n, CH])
                        say(gp.tensor_tensor(EM[:].rearrange("q c p k t -> q (c p) k t")[:, lo:lo + n, j, :], e_, m_, ALU.mult), "EM")
                blocks_below(0, 4)
                on(gp, layer, "gdn_rows")
                on(gp, layer, "KQ")
                say(gp.memset(At[:], 0.0), "At_zero")
                blocks_below(1, 0)
                blocks_below(1, 1)
                blocks_below(0, 5)
                gla_keys(1)
                gla_keys(2)
                blocks_below(1, 2)
                gla_keys(3)
                blocks_below(1, 3)
                gla_keys(4)
                gla_keys(5)
                blocks_below(1, 4)
                gla_keys(6)
                on(gp, layer, "xc")
                say(kept(rgp, 3, "rgc", 2), "rgc_kept")
                blocks_below(1, 5)
                on(gp, layer, "rg_h")
                ho = so[:, SOUT["h"][0]:SOUT["h"][0] + 18].rearrange("q (p s) -> q p s", p=2)
                st(gp.tensor_copy(ho[:, :, 0], ri[:, :, SEQ - 1]))
                say(gp.tensor_copy(ho[:, :, 1:], seqs(ri, 0, DECT - 1, 1).rearrange("q p s t -> q p (s t)")), "rg_kept")
                on(gp, layer, "o_lo", 1)
                sm = C("seqm").unsqueeze(2).broadcast_to([128, DECB, 64])
                for g in range(3):
                    if g == 0:
                        on(gp, layer, "rg_kept")
                        on(gp, layer, "rU")
                        on(gp, layer, "gU")
                        srcs = ((VM, rVt), (UM, UU[0]))
                    elif g == 1:
                        on(gp, layer, "dec_mm", 1)
                        srcs = ((UM, UU[1]),)
                    else:
                        srcs = ((VM, lVt),)
                    for j, (dst, src) in enumerate(srcs):
                        for p in range(2):
                            ins = gp.tensor_tensor(dst[:, p], src[:, DEC, p, :].unsqueeze(1).broadcast_to([128, DECB, 64]), sm, ALU.mult)
                            say(ins, "VM") if j == len(srcs) - 1 else st(ins)
                    on(gp, layer, "out_mm", g + 1)
                    if g < 2:
                        for p in range(2):
                            v = (Mrw, Mgdn)[g][:, p, 1:, :]
                            d_ = seqs((rP, eG)[g][:, p, :], 0)[:, :, DECT - 1:DECT].broadcast_to([128, DECB, 64])
                            ins = gp.tensor_tensor(v, v, d_, ALU.mult)
                            say(ins, "dec_decay") if p else st(ins)
                    else:
                        v = Mgla[:, 1:, :]
                        d_ = seqs(lB, 0)[:, :, DECT - 1:DECT].broadcast_to([128, DECB, 64])
                        say(gp.tensor_tensor(v, v, d_, ALU.mult), "dec_decay")
                apart(gp, state_out, layer * 32 + 32)

        for s in [v_step, a_step, g_step, in_read] + list(S.values()):
            assert s.given == s.n, (s.name, s.given)


INS = ("xT", "wts", "par", "cst", "sin", "mst")
OUTS = {"yT": [128, KT, TOK], "sout": [DEPTH, 128, SOUTN], "mout": [DEPTH, 128, MSTN]}


def declare(nc):
    shapes = {"xT": [128, KT, TOK], "wts": [DEPTH * UNITS, 128, 1024], "par": [DEPTH, 128, PARN], "cst": [128, CSTN],
              "sin": [DEPTH, 128, SINN], "mst": [DEPTH, 128, MSTN]}
    args = [nc.dram_tensor(n, shapes[n], F32, kind="ExternalInput").ap() for n in INS]
    args += [nc.dram_tensor(n, s, F32, kind="ExternalOutput").ap() for n, s in OUTS.items()]
    program(nc, *args)


def constants(norm_final):
    c = np.zeros((128, CSTN), np.float32)

    def put(name, a):
        at, n = CST[name]
        c[:, at:at + n] = np.asarray(a, np.float32).reshape(-1, n)

    q, j = np.arange(128), np.arange(64)
    same = (q[:, None] // 64 == q[None, :] // 64)
    put("hones", same)
    put("ones", np.ones((128, 128)))
    s, t = (q % 64)[:, None], j[None, :]
    block = s // DECT == t // DECT
    put("tri", np.stack([s < t, s <= t, (s < t) & block, (s <= t) & block], 1).reshape(128, -1))
    lev = [s == t]
    for l in range(6):
        w = 1 << l
        lev.append((s // (2 * w) == t // (2 * w)) & (s % (2 * w) < w) & (t % (2 * w) >= w))
    put("lev", np.stack(lev, 1).reshape(128, -1))
    tok = np.arange(TOK)
    put("cmask", np.tile(np.where(tok < SEQ, tok % CH, (tok - SEQ) % DECT) != 0, (128, 1)))
    put("seqm", (q % 64)[:, None] // DECT == np.arange(DECB)[None])
    for name, v in (("e6", 1e-6), ("e12", 1e-12), ("gne", GNE), ("one", 1.0)):
        put(name, np.full((128, 1), v))
    at, n = CST["nf"]
    c[:, at:at + n] = norm_final.reshape(KT, 128).T
    return c


def tiles(a):
    return np.moveaxis(a.reshape(*a.shape[:-1], -1, 128), -1, -2)


def lay_out(i):
    i = {k: np.asarray(v) for k, v in i.items()}
    L = DEPTH
    x = np.concatenate([i["x_prompt"][0], i["x_sample"].reshape(-1, D)])
    xT = x.T.reshape(KT, 128, TOK).transpose(1, 0, 2)

    def cols(w):
        return w.reshape(KT, 128, -1, 128).transpose(2, 1, 0, 3).reshape(-1, 128, 1024)

    wts = []
    for l in range(L):
        def ffn(n):
            g, u = cols(i[f"ffn{n}_gate"][l]), cols(i[f"ffn{n}_up"][l])
            return [np.stack([g, u], 1).reshape(-1, 128, 1024), i[f"ffn{n}_down"][l].reshape(FT, 128, 1024)]
        w = i["w_in"][l]
        tw = np.zeros((D, IN_TILES * 128), np.float32)
        for m, at in enumerate(TILE_COL):
            if at is not None:
                tw[:, m * 128:m * 128 + 128] = w[:, at:at + 128]
        b0 = GDN0 + 4 * GW
        for at, src, n in ((0, b0, NH), (32, b0 + NH, NH), (64, GLA_GD, 16)):
            tw[:, T_SMALL * 128 + at:T_SMALL * 128 + at + n] = w[:, src:src + n]
        wts += ffn(1) + [cols(tw), cols(i["w_out"][l])] + ffn(2)
    wts = np.concatenate(wts)

    par = np.zeros((L, 128, PARN), np.float32)

    def put(name, a):
        at, n = PAR[name]
        par[:, :, at:at + n] = a.reshape(L, 128, n)

    for name, key in (("n1", "norm_ffn1"), ("nm", "norm_mix"), ("n2", "norm_ffn2"), ("mu", "rwkv_mu"), ("w0", "rwkv_w0"),
                      ("a0", "rwkv_a0"), ("kk", "rwkv_k_k"), ("ka", "rwkv_k_a"), ("lnw", "rwkv_ln_w"), ("lnb", "rwkv_ln_b"),
                      ("rgcb", "rg_conv_b"), ("ba", "rg_ba"), ("bx", "rg_bx"), ("lam", "rg_lambda"), ("gb", "gla_gb")):
        put(name, tiles(i[key]))
    put("rk", tiles(i["rwkv_r_k"].reshape(L, GW)))
    for name, key in (("rgcw", "rg_conv_w"), ("gcw", "gdn_conv_w")):
        put(name, tiles(i[key]).transpose(0, 2, 1, 3))
    for name, key in (("gnw", "gdn_norm_w"), ("glw", "gla_norm_w")):
        put(name, np.concatenate([i[key], i[key]], 1))
    for name, key in (("alog", "gdn_A_log"), ("dtb", "gdn_dt_bias")):
        par[:, 32:32 + NH, PAR[name][0]] = i[key]
    put("lora", np.concatenate([i["rwkv_w2"], i["rwkv_a2"], i["rwkv_g2"]], 1))
    par[:, 64:80, PAR["glag"][0]:PAR["glag"][0] + 128] = i["gla_g2"]
    for h in range(NH):
        at = PAR["glag"][0] + 64 * h
        par[:, h, at:at + 64] = par[:, 32 + h, at:at + 64] = 1
    for name, key in (("wa", "rg_wa"), ("wx", "rg_wx")):
        for h in range(NH):
            b, p = h % 2, h // 2
            at = PAR[name][0] + 64 * p
            par[:, 64 * b:64 * b + 64, at:at + 64] = i[key][:, h]

    def rows(a, k, n):
        return a.reshape(L, DECB, n, k, 128).transpose(0, 4, 3, 1, 2).reshape(L, 128, -1)

    sin = np.concatenate([rows(i["state_rwkv_shift"], 7, 1), rows(i["state_rglru_conv"], 2, 3), rows(i["state_rglru_h"], 2, 1),
                          rows(i["state_gdn_conv"], 6, 3)], 2)
    mst = np.zeros((L, 128, MSTN), np.float32)

    for name, a in (("rw", i["state_rwkv_wkv"].transpose(0, 1, 2, 4, 3)), ("gdn", i["state_gdn_S"]), ("gla", i["state_gla_S"])):
        at, n = MST[name]
        p = n // NSEQ // 64
        full = np.zeros((L, 128, p, NSEQ, 64), np.float32)
        full[:, :, :, 1:] = a.reshape(L, DECB, p, 128, 64).transpose(0, 3, 2, 1, 4)
        mst[:, :, at:at + n] = full.reshape(L, 128, n)
    return dict(xT=xT, wts=wts, par=par, cst=constants(i["norm_final"]), sin=sin, mst=mst)


def take_back(r):
    y = r["yT"].transpose(1, 0, 2).reshape(D, TOK).T
    L = DEPTH
    so, mo = r["sout"], r["mout"]

    def small_of(name, k, n):
        at, w = SOUT[name]
        a = so[:, :, at:at + w].reshape(L, 128, k, NSEQ, n).transpose(0, 3, 4, 2, 1).reshape(L, NSEQ, n, k * 128)
        return a[:, :, 0] if n == 1 else a

    def matrix_of(name, dk):
        at, w = MST[name]
        p = w // NSEQ // 64
        return mo[:, :, at:at + w].reshape(L, 128, p, NSEQ, 64).transpose(0, 3, 2, 1, 4).reshape(L, NSEQ, NH, dk, 64)

    st = [small_of("shift", 7, 1), matrix_of("rw", 64).transpose(0, 1, 2, 4, 3), small_of("rgc", 2, 3), small_of("h", 2, 1),
          small_of("gc", 6, 3), matrix_of("gdn", 64), matrix_of("gla", DK)]
    c = np.ascontiguousarray
    return tuple([c(y[:SEQ].reshape(1, SEQ, D)), c(y[SEQ:].reshape(DECB, DECT, D))]
                 + [c(s[:, :1]) for s in st] + [c(s[:, 1:]) for s in st])


def kernel(**inputs):
    import concourse.bacc as bacc
    from concourse.bass_utils import run_bass_kernel_spmd
    nc = bacc.Bacc("TRN2", target_bir_lowering=False, num_devices=1)
    declare(nc)
    arrays = {k: np.ascontiguousarray(v) for k, v in lay_out(inputs).items()}
    r = run_bass_kernel_spmd(nc, [arrays], core_ids=[0])
    return take_back(r.results[0])
```
